# Optimizing a Trainium2 kernel written in Bass

```python
import math
import jax, jax.numpy as jnp
from jax import lax
import numpy as np

D_MODEL = 1024
BATCH = 1
SEQ = 1024
DEPTH = 1

CTX_LEN = 256
GRID_W = 64

SSD_HEADS = 16
SSD_HEAD_DIM = 64
D_SSD = SSD_HEADS * SSD_HEAD_DIM
SSD_GROUPS = 2
SSD_HEADS_PER_GROUP = SSD_HEADS // SSD_GROUPS
D_STATE = 128
CONV_W = 5
CHUNK = 128
D_XBC = D_SSD + 2 * SSD_GROUPS * D_STATE

ATTN_Q_HEADS = 16
ATTN_KV_HEADS = 4
HEAD_DIM = 64
GQA_GROUP = ATTN_Q_HEADS // ATTN_KV_HEADS
D_ATTN = ATTN_Q_HEADS * HEAD_DIM
ROPE_THETA = 10000.0
Q_BLOCK = 128

D_MIX = D_SSD + D_ATTN

OFF_Z = 0
OFF_Q = OFF_Z + D_SSD
OFF_XBC = OFF_Q + D_ATTN
OFF_DT = OFF_XBC + D_XBC
OFF_K = OFF_DT + 2 * SSD_HEADS
OFF_V = OFF_K + ATTN_KV_HEADS * HEAD_DIM
D_IN_PROJ = OFF_V + ATTN_KV_HEADS * HEAD_DIM

MOE_GROUPS = 4
EXPERTS_PER_GROUP = 4
N_EXPERTS = MOE_GROUPS * EXPERTS_PER_GROUP
TOP_K_IN_GROUP = 2
D_EXPERT = 256


F32 = jnp.float32

def layer_norm(x, g, b, eps=1e-5):
    xf = x.astype(F32)
    mu = jnp.mean(xf, -1, keepdims=True)
    var = jnp.mean(jnp.square(xf - mu), -1, keepdims=True)
    return ((xf - mu) * lax.rsqrt(var + eps) * g + b).astype(x.dtype)

def rms_norm(x, g, eps=1e-6):
    xf = x.astype(F32)
    return (xf * lax.rsqrt(jnp.mean(xf * xf, -1, keepdims=True) + eps) * g).astype(x.dtype)

def dwconv_silu(u, w, b):
    y = lax.conv_general_dilated(u, w[:, None, :], (1,), [(CONV_W // 2, CONV_W // 2)],
                                 dimension_numbers=('NWC', 'WIO', 'NWC'),
                                 feature_group_count=u.shape[-1])
    return jax.nn.silu(y + b)

def axial_rope_tables(n_rows):
    rows = jnp.broadcast_to(jnp.arange(n_rows, dtype=F32)[:, None], (n_rows, GRID_W)).reshape(-1)
    cols = jnp.broadcast_to(jnp.arange(GRID_W, dtype=F32)[None, :], (n_rows, GRID_W)).reshape(-1)
    axis_dim = HEAD_DIM // 2
    inv_freq = jnp.power(ROPE_THETA, -jnp.arange(0, axis_dim, 2, dtype=F32) / axis_dim)
    ang = jnp.concatenate([rows[:, None] * inv_freq, cols[:, None] * inv_freq], -1)
    return jnp.cos(ang), jnp.sin(ang)

def apply_rope(x, cos, sin):
    xf = x.astype(F32).reshape(*x.shape[:-1], HEAD_DIM // 2, 2)
    x0, x1 = xf[..., 0], xf[..., 1]
    c = cos[None, :, None, :]
    s = sin[None, :, None, :]
    out = jnp.stack([x0 * c - x1 * s, x0 * s + x1 * c], -1)
    return out.reshape(x.shape).astype(x.dtype)

def ssd_scan(xs, dt, A, Bm, Cm, h0, with_output):
    b, L = xs.shape[:2]
    nc = L // CHUNK
    G, R, P, N = SSD_GROUPS, SSD_HEADS_PER_GROUP, SSD_HEAD_DIM, D_STATE
    xdt = (xs.astype(F32) * dt[..., None]).reshape(b, nc, CHUNK, G, R, P)
    a_cs = jnp.cumsum((dt * A).reshape(b, nc, CHUNK, G, R), axis=2)
    Bc = Bm.astype(F32).reshape(b, nc, CHUNK, G, N)
    w_state = jnp.exp(a_cs[:, :, -1:] - a_cs)
    chunk_states = jnp.einsum('bcsgn,bcsgr,bcsgrp->bcgrpn', Bc, w_state, xdt)
    chunk_decay = jnp.exp(a_cs[:, :, -1])

    def carry_state(h, inp):
        s_c, d_c = inp
        return h * d_c[..., None, None] + s_c, h

    h_final, h_in = lax.scan(carry_state, h0,
                             (jnp.moveaxis(chunk_states, 1, 0), jnp.moveaxis(chunk_decay, 1, 0)))
    if not with_output:
        return h_final
    Cc = Cm.astype(F32).reshape(b, nc, CHUNK, G, N)
    diff = a_cs[:, :, :, None] - a_cs[:, :, None]
    lower = jnp.tril(jnp.ones((CHUNK, CHUNK), bool))[:, :, None, None]
    decay = jnp.where(lower, jnp.exp(jnp.where(lower, diff, 0.0)), 0.0)
    cb = jnp.einsum('bcqgn,bcsgn->bcqsg', Cc, Bc)
    y_diag = jnp.einsum('bcqsgr,bcsgrp->bcqgrp', cb[..., None] * decay, xdt)
    y_off = jnp.einsum('bcqgn,bcgrpn,bcqgr->bcqgrp', Cc, jnp.moveaxis(h_in, 0, 1), jnp.exp(a_cs))
    return (y_diag + y_off).reshape(b, L, G, R, P), h_final

def ssd_bidirectional(xs, Bm, Cm, dt, A, h0_f, h0_b, with_output):
    fl = lambda u: jnp.flip(u, axis=1)
    out_f = ssd_scan(xs, dt[:, :, 0], A[0], Bm, Cm, h0_f, with_output)
    out_b = ssd_scan(fl(xs), fl(dt[:, :, 1]), A[1], fl(Bm), fl(Cm), h0_b, with_output)
    return out_f, out_b

def ssd_prepare(xbc_raw, dt_raw, p):
    b, L, _ = xbc_raw.shape
    xbc = dwconv_silu(xbc_raw, p['conv_w'], p['conv_b'])
    gn = SSD_GROUPS * D_STATE
    xs = xbc[..., :D_SSD].reshape(b, L, SSD_GROUPS, SSD_HEADS_PER_GROUP, SSD_HEAD_DIM)
    Bm = xbc[..., D_SSD:D_SSD + gn].reshape(b, L, SSD_GROUPS, D_STATE)
    Cm = xbc[..., D_SSD + gn:].reshape(b, L, SSD_GROUPS, D_STATE)
    dt = jax.nn.softplus(dt_raw.astype(F32).reshape(b, L, 2, SSD_HEADS) + p['dt_bias'].astype(F32))
    dt = dt.reshape(b, L, 2, SSD_GROUPS, SSD_HEADS_PER_GROUP)
    A = -jnp.exp(p['a_log'].astype(F32)).reshape(2, SSD_GROUPS, SSD_HEADS_PER_GROUP)
    return xs, Bm, Cm, dt, A

def ssd_output(y_f, y_b, xs, z, p):
    b, L = z.shape[:2]
    skip = p['d_skip'].astype(F32).reshape(SSD_GROUPS, SSD_HEADS_PER_GROUP)[..., None]
    y = y_f + jnp.flip(y_b, axis=1) + xs.astype(F32) * skip
    y = y.reshape(b, L, D_SSD) * jax.nn.silu(z.astype(F32))
    yg = y.reshape(b, L, SSD_GROUPS, D_SSD // SSD_GROUPS)
    yg = yg * lax.rsqrt(jnp.mean(yg * yg, -1, keepdims=True) + 1e-6)
    return (yg.reshape(b, L, D_SSD) * p['ssd_norm_g']).astype(z.dtype)

def gqa_block_attention(q, k, v):
    b, L = q.shape[:2]
    nblk = L // Q_BLOCK
    qb = q.reshape(b, nblk, Q_BLOCK, ATTN_KV_HEADS, GQA_GROUP, HEAD_DIM).swapaxes(0, 1)
    scale = HEAD_DIM ** -0.5

    def one_block(q_blk):
        s = jnp.einsum('bqhgd,bkhd->bhgqk', q_blk, k, preferred_element_type=F32) * scale
        pr = jax.nn.softmax(s, axis=-1).astype(v.dtype)
        return jnp.einsum('bhgqk,bkhd->bqhgd', pr, v)

    o = lax.map(one_block, qb)
    return o.swapaxes(0, 1).reshape(b, L, D_ATTN)

def context_mixer(hc, p, with_output):
    b, S, _ = hc.shape
    side = hc @ p['w_in'][:, OFF_XBC:]
    xbc_raw = side[..., :OFF_DT - OFF_XBC]
    dt_raw = side[..., OFF_DT - OFF_XBC:OFF_K - OFF_XBC]
    k = rms_norm(side[..., OFF_K - OFF_XBC:OFF_V - OFF_XBC].reshape(b, S, ATTN_KV_HEADS, HEAD_DIM), p['k_norm_g'])
    v = side[..., OFF_V - OFF_XBC:].reshape(b, S, ATTN_KV_HEADS, HEAD_DIM)
    xs, Bm, Cm, dt, A = ssd_prepare(xbc_raw, dt_raw, p)
    h0 = jnp.zeros((b, SSD_GROUPS, SSD_HEADS_PER_GROUP, SSD_HEAD_DIM, D_STATE), F32)
    if not with_output:
        hf, hb = ssd_bidirectional(xs, Bm, Cm, dt, A, h0, h0, False)
        return (k, v, hf, hb), None
    (y_f, hf), (y_b, hb) = ssd_bidirectional(xs, Bm, Cm, dt, A, h0, h0, True)
    zq = hc @ p['w_in'][:, :OFF_XBC]
    z = zq[..., OFF_Z:OFF_Q]
    q = rms_norm(zq[..., OFF_Q:].reshape(b, S, ATTN_Q_HEADS, HEAD_DIM), p['q_norm_g'])
    y_ssd = ssd_output(y_f, y_b, xs, z, p)
    o = gqa_block_attention(q, k, v)
    return (k, v, hf, hb), jnp.concatenate([y_ssd, o], -1) @ p['w_out']

def latent_mixer(hx, ctx_side, p, cos, sin):
    b, L, _ = hx.shape
    k_ctx, v_ctx, hf_ctx, hb_ctx = ctx_side
    proj = hx @ p['w_in']
    z = proj[..., OFF_Z:OFF_Q]
    q = proj[..., OFF_Q:OFF_XBC].reshape(b, L, ATTN_Q_HEADS, HEAD_DIM)
    xbc_raw = proj[..., OFF_XBC:OFF_DT]
    dt_raw = proj[..., OFF_DT:OFF_K]
    k = proj[..., OFF_K:OFF_V].reshape(b, L, ATTN_KV_HEADS, HEAD_DIM)
    v = proj[..., OFF_V:].reshape(b, L, ATTN_KV_HEADS, HEAD_DIM)
    xs, Bm, Cm, dt, A = ssd_prepare(xbc_raw, dt_raw, p)
    (y_f, _), (y_b, _) = ssd_bidirectional(xs, Bm, Cm, dt, A, hf_ctx, hb_ctx, True)
    y_ssd = ssd_output(y_f, y_b, xs, z, p)
    q = apply_rope(rms_norm(q, p['q_norm_g']), cos, sin)
    k = apply_rope(rms_norm(k, p['k_norm_g']), cos, sin)
    o = gqa_block_attention(q, jnp.concatenate([k_ctx, k], axis=1), jnp.concatenate([v_ctx, v], axis=1))
    return jnp.concatenate([y_ssd, o], -1) @ p['w_out']

def hier_moe(h, p):
    b, L, d = h.shape
    t = h.reshape(-1, d)
    g_prob = jax.nn.softmax((t @ p['w_rg'] + p['b_rg']).astype(F32), axis=-1)
    g_val, g_idx = lax.top_k(g_prob, 1)
    e_logits = (t @ p['w_re'] + p['b_re']).astype(F32).reshape(-1, MOE_GROUPS, EXPERTS_PER_GROUP)
    e_sel = jnp.take_along_axis(e_logits, g_idx[:, :, None], axis=1)[:, 0]
    e_val, e_idx = lax.top_k(jax.nn.softmax(e_sel, axis=-1), TOP_K_IN_GROUP)
    e_val = e_val / jnp.sum(e_val, -1, keepdims=True)
    w_group = jnp.sum(jax.nn.one_hot(e_idx, EXPERTS_PER_GROUP, dtype=F32) * e_val[..., None], axis=1)
    combine = jax.nn.one_hot(g_idx[:, 0], MOE_GROUPS, dtype=F32)[:, :, None] * g_val[:, :, None] * w_group[:, None, :]
    combine = combine.reshape(-1, N_EXPERTS).astype(t.dtype)
    gate = jnp.einsum('td,edf->tef', t, p['w_gate'])
    up = jnp.einsum('td,edf->tef', t, p['w_up'])
    hid = jax.nn.silu(gate) * up * combine[..., None]
    return jnp.einsum('tef,efd->td', hid, p['w_down']).reshape(b, L, d)

def first_inputs(seed: int = 0) -> dict:
    key = jax.random.key(seed)
    ks = jax.random.split(key, 28)
    nrm = lambda k, shape, scale: jax.random.normal(k, shape, F32) * scale
    beta = (8.0 * DEPTH) ** -0.25
    dt0 = jnp.exp(jax.random.uniform(ks[9], (DEPTH, 2, SSD_HEADS), F32, math.log(1e-3), math.log(1e-1)))
    dt_bias = dt0 + jnp.log(-jnp.expm1(-dt0))
    a_log = jnp.log(jax.random.uniform(ks[10], (DEPTH, 2, SSD_HEADS), F32, 1.0, 16.0))
    return {
        'x': nrm(ks[0], (BATCH, SEQ, D_MODEL), 1.0),
        'c': nrm(ks[1], (BATCH, D_MODEL), 1.0),
        'ctx': nrm(ks[2], (BATCH, CTX_LEN, D_MODEL), 1.0),
        'c_ctx': nrm(ks[3], (D_MODEL,), 1.0),
        'w_mod': nrm(ks[4], (DEPTH, D_MODEL, 6 * D_MODEL), 0.5 * D_MODEL ** -0.5),
        'b_mod': nrm(ks[5], (DEPTH, 6 * D_MODEL), 0.02),
        'w_in': nrm(ks[6], (DEPTH, D_MODEL, D_IN_PROJ), D_MODEL ** -0.5),
        'conv_w': nrm(ks[7], (DEPTH, CONV_W, D_XBC), CONV_W ** -0.5),
        'conv_b': nrm(ks[8], (DEPTH, D_XBC), 0.02),
        'dt_bias': dt_bias,
        'a_log': a_log,
        'd_skip': 1.0 + nrm(ks[11], (DEPTH, SSD_HEADS), 0.05),
        'ssd_norm_g': 1.0 + nrm(ks[12], (DEPTH, D_SSD), 0.05),
        'q_norm_g': 1.0 + nrm(ks[13], (DEPTH, HEAD_DIM), 0.05),
        'k_norm_g': 1.0 + nrm(ks[14], (DEPTH, HEAD_DIM), 0.05),
        'w_out': nrm(ks[15], (DEPTH, D_MIX, D_MODEL), beta * D_MIX ** -0.5),
        'ln1_g': 1.0 + nrm(ks[16], (DEPTH, D_MODEL), 0.05),
        'ln1_b': nrm(ks[17], (DEPTH, D_MODEL), 0.02),
        'w_rg': nrm(ks[18], (DEPTH, D_MODEL, MOE_GROUPS), D_MODEL ** -0.5),
        'b_rg': nrm(ks[19], (DEPTH, MOE_GROUPS), 0.01),
        'w_re': nrm(ks[20], (DEPTH, D_MODEL, N_EXPERTS), D_MODEL ** -0.5),
        'b_re': nrm(ks[21], (DEPTH, N_EXPERTS), 0.01),
        'w_gate': nrm(ks[22], (DEPTH, N_EXPERTS, D_MODEL, D_EXPERT), D_MODEL ** -0.5),
        'w_up': nrm(ks[23], (DEPTH, N_EXPERTS, D_MODEL, D_EXPERT), D_MODEL ** -0.5),
        'w_down': nrm(ks[24], (DEPTH, N_EXPERTS, D_EXPERT, D_MODEL), beta * D_EXPERT ** -0.5),
        'ln2_g': 1.0 + nrm(ks[25], (DEPTH, D_MODEL), 0.05),
        'ln2_b': nrm(ks[26], (DEPTH, D_MODEL), 0.02),
    }

def first_block(x, c, ctx, c_ctx, w_mod, b_mod, w_in, conv_w, conv_b, dt_bias, a_log, d_skip, ssd_norm_g,
              q_norm_g, k_norm_g, w_out, ln1_g, ln1_b, w_rg, b_rg, w_re, b_re, w_gate, w_up, w_down,
              ln2_g, ln2_b):
    n_rows = x.shape[1] // GRID_W
    cos, sin = axial_rope_tables(n_rows)
    alpha = (2.0 * DEPTH) ** 0.25
    silu_c = jax.nn.silu(c)
    silu_cc = jax.nn.silu(c_ctx)
    for l in range(DEPTH):
        last = l == DEPTH - 1
        p = {'w_in': w_in[l], 'conv_w': conv_w[l], 'conv_b': conv_b[l], 'dt_bias': dt_bias[l],
             'a_log': a_log[l], 'd_skip': d_skip[l], 'ssd_norm_g': ssd_norm_g[l], 'q_norm_g': q_norm_g[l],
             'k_norm_g': k_norm_g[l], 'w_out': w_out[l], 'w_rg': w_rg[l], 'b_rg': b_rg[l], 'w_re': w_re[l],
             'b_re': b_re[l], 'w_gate': w_gate[l], 'w_up': w_up[l], 'w_down': w_down[l]}
        sh_a, sc_a, g_a, sh_f, sc_f, g_f = [m[:, None, :] for m in jnp.split(silu_c @ w_mod[l] + b_mod[l], 6, axis=-1)]
        n_mod = 3 if last else 6
        mod_c = jnp.split(silu_cc @ w_mod[l][:, :n_mod * D_MODEL] + b_mod[l][:n_mod * D_MODEL], n_mod, axis=-1)
        hc = ctx * (1.0 + mod_c[1]) + mod_c[0]
        ctx_side, ctx_out = context_mixer(hc, p, not last)
        hx = x * (1.0 + sc_a) + sh_a
        x = layer_norm(alpha * x + g_a * latent_mixer(hx, ctx_side, p, cos, sin), ln1_g[l], ln1_b[l])
        x = layer_norm(alpha * x + g_f * hier_moe(x * (1.0 + sc_f) + sh_f, p), ln2_g[l], ln2_b[l])
        if not last:
            ctx = layer_norm(alpha * ctx + mod_c[2] * ctx_out, ln1_g[l], ln1_b[l])
            ctx = layer_norm(alpha * ctx + mod_c[5] * hier_moe(ctx * (1.0 + mod_c[4]) + mod_c[3], p),
                             ln2_g[l], ln2_b[l])
    return x


D_MIX_2 = D_MODEL
D_POOL = D_MIX_2 // 2
D_SSM = D_MIX_2 - D_POOL
POOL_WINDOWS = (2, 4, 8, 16)
N_POOL_GROUPS = len(POOL_WINDOWS)
POOL_GROUP = D_POOL // N_POOL_GROUPS
SSM_GROUP = 16
N_SSM_GROUPS = D_SSM // SSM_GROUP
SSM_STATE = 64
D_FF = -(-8 * D_MODEL // (3 * 256)) * 256
RMS_EPS = 1e-6
DT_MIN = 1e-3
DT_MAX = 1e-1


def rmsnorm(x, g):
    xf = x.astype(jnp.float32)
    y = xf * lax.rsqrt(jnp.mean(xf * xf, axis=-1, keepdims=True) + RMS_EPS)
    return y.astype(x.dtype) * g

def pool_mixer(u, w_pool, scale):
    b, l, _ = u.shape
    ug = u.astype(jnp.float32).reshape(b, l, N_POOL_GROUPS, POOL_GROUP)
    cs = jnp.cumsum(ug, axis=1)
    n_pos = jnp.arange(1, l + 1, dtype=jnp.float32)
    diffs = []
    for gi, w in enumerate(POOL_WINDOWS):
        c = cs[:, :, gi]
        lagged = jnp.pad(c, ((0, 0), (w, 0), (0, 0)))[:, :l]
        mean = (c - lagged) / jnp.minimum(n_pos, float(w))[None, :, None]
        diffs.append(mean - ug[:, :, gi])
    d = jnp.stack(diffs, axis=2)
    y = jnp.einsum('blgc,gcd->blgd', d, w_pool.astype(jnp.float32)).reshape(b, l, D_POOL)
    return (y * scale.astype(jnp.float32)).astype(u.dtype)

def _complex_affine_combine(e1, e2):
    a1r, a1i, b1r, b1i = e1
    a2r, a2i, b2r, b2i = e2
    ar = a2r * a1r - a2i * a1i
    ai = a2r * a1i + a2i * a1r
    br = a2r * b1r - a2i * b1i + b2r
    bi = a2r * b1i + a2i * b1r + b2i
    return ar, ai, br, bi

def ssm_mixer(u, lam_re, lam_im, log_dt, b_re, b_im, c_re, c_im, d_skip, w_glu, b_glu):
    f32 = jnp.float32
    bsz, l, _ = u.shape
    ug = u.astype(f32).reshape(bsz, l, N_SSM_GROUPS, SSM_GROUP)
    lr, li = lam_re.astype(f32), lam_im.astype(f32)
    dt = jnp.exp(log_dt.astype(f32))[:, None]
    mag = jnp.exp(lr * dt)
    abar_r = mag * jnp.cos(li * dt)
    abar_i = mag * jnp.sin(li * dt)
    den = lr * lr + li * li
    nr, ni = abar_r - 1.0, abar_i
    coef_r = (nr * lr + ni * li) / den
    coef_i = (ni * lr - nr * li) / den
    br, bi = b_re.astype(f32), b_im.astype(f32)
    bbar_r = coef_r[..., None] * br - coef_i[..., None] * bi
    bbar_i = coef_r[..., None] * bi + coef_i[..., None] * br
    bu_r = jnp.einsum('blgh,gph->blgp', ug, bbar_r)
    bu_i = jnp.einsum('blgh,gph->blgp', ug, bbar_i)
    a_r = jnp.broadcast_to(abar_r, (1, l, N_SSM_GROUPS, SSM_STATE))
    a_i = jnp.broadcast_to(abar_i, (1, l, N_SSM_GROUPS, SSM_STATE))
    _, _, s_r, s_i = lax.associative_scan(_complex_affine_combine, (a_r, a_i, bu_r, bu_i), axis=1)
    y = (jnp.einsum('blgp,ghp->blgh', s_r, c_re.astype(f32))
         - jnp.einsum('blgp,ghp->blgh', s_i, c_im.astype(f32))
         + d_skip.astype(f32) * ug).reshape(bsz, l, D_SSM)
    y = jax.nn.gelu(y)
    y = y * jax.nn.sigmoid(y @ w_glu.astype(f32) + b_glu.astype(f32))
    return y.astype(u.dtype)

def swiglu(h, w_gate, w_up, w_down):
    return (jax.nn.silu(h @ w_gate) * (h @ w_up)) @ w_down

def second_inputs(seed: int = 0) -> dict:
    key = jax.random.key(seed)
    ks = jax.random.split(key, 24)
    f32 = jnp.float32
    nrm = lambda k, s, sc: jax.random.normal(k, s, f32) * sc
    res_scale = (2 * DEPTH) ** -0.5
    n_idx = jnp.arange(SSM_STATE, dtype=f32)
    lam_re = -0.5 + nrm(ks[5], (DEPTH, N_SSM_GROUPS, SSM_STATE), 0.01)
    lam_im = math.pi * n_idx[None, None, :] + nrm(ks[6], (DEPTH, N_SSM_GROUPS, SSM_STATE), 0.01)
    log_dt = jax.random.uniform(ks[7], (DEPTH, N_SSM_GROUPS), f32, math.log(DT_MIN), math.log(DT_MAX))
    return {
        "x": nrm(ks[0], (BATCH, SEQ, D_MODEL), 1.0),
        "norm_mix": 1.0 + nrm(ks[1], (DEPTH, D_MODEL), 0.02),
        "w_in": nrm(ks[2], (DEPTH, D_MODEL, D_MIX_2), D_MODEL ** -0.5),
        "w_pool": nrm(ks[3], (DEPTH, N_POOL_GROUPS, POOL_GROUP, POOL_GROUP), POOL_GROUP ** -0.5),
        "pool_scale": 1.0 + nrm(ks[4], (DEPTH, D_POOL), 0.02),
        "lam_re": lam_re,
        "lam_im": lam_im,
        "log_dt": log_dt,
        "b_re": nrm(ks[8], (DEPTH, N_SSM_GROUPS, SSM_STATE, SSM_GROUP), (2 * SSM_GROUP) ** -0.5),
        "b_im": nrm(ks[9], (DEPTH, N_SSM_GROUPS, SSM_STATE, SSM_GROUP), (2 * SSM_GROUP) ** -0.5),
        "c_re": nrm(ks[10], (DEPTH, N_SSM_GROUPS, SSM_GROUP, SSM_STATE), (2 * SSM_STATE) ** -0.5),
        "c_im": nrm(ks[11], (DEPTH, N_SSM_GROUPS, SSM_GROUP, SSM_STATE), (2 * SSM_STATE) ** -0.5),
        "d_skip": nrm(ks[12], (DEPTH, N_SSM_GROUPS, SSM_GROUP), 1.0),
        "w_glu": nrm(ks[13], (DEPTH, D_SSM, D_SSM), D_SSM ** -0.5),
        "b_glu": nrm(ks[14], (DEPTH, D_SSM), 0.01),
        "w_out": nrm(ks[15], (DEPTH, D_MIX_2, D_MODEL), D_MIX_2 ** -0.5 * res_scale),
        "norm_ffn": 1.0 + nrm(ks[16], (DEPTH, D_MODEL), 0.02),
        "w_gate": nrm(ks[17], (DEPTH, D_MODEL, D_FF), D_MODEL ** -0.5),
        "w_up": nrm(ks[18], (DEPTH, D_MODEL, D_FF), D_MODEL ** -0.5),
        "w_down": nrm(ks[19], (DEPTH, D_FF, D_MODEL), D_FF ** -0.5 * res_scale),
        "norm_final": 1.0 + nrm(ks[20], (D_MODEL,), 0.02),
    }

def second_block(x, norm_mix, w_in, w_pool, pool_scale, lam_re, lam_im, log_dt, b_re, b_im,
              c_re, c_im, d_skip, w_glu, b_glu, w_out, norm_ffn, w_gate, w_up, w_down,
              norm_final):
    h = x
    for i in range(DEPTH):
        u = rmsnorm(h, norm_mix[i]) @ w_in[i]
        u_pool, u_ssm = u[..., :D_POOL], u[..., D_POOL:]
        y_pool = pool_mixer(u_pool, w_pool[i], pool_scale[i])
        y_ssm = ssm_mixer(u_ssm, lam_re[i], lam_im[i], log_dt[i], b_re[i], b_im[i],
                          c_re[i], c_im[i], d_skip[i], w_glu[i], b_glu[i])
        h = h + jnp.concatenate([y_pool, y_ssm], axis=-1) @ w_out[i]
        h = h + swiglu(rmsnorm(h, norm_ffn[i]), w_gate[i], w_up[i], w_down[i])
    return rmsnorm(h, norm_final)


def setup_inputs(seed=0):
    out = dict(first_inputs(seed))
    for name, value in second_inputs(seed + 1).items():
        if name != "x":
            out[name + "_2"] = value
    return out


def reference(
    x, c, ctx, c_ctx, w_mod, b_mod, w_in, conv_w, conv_b, dt_bias, a_log, d_skip, ssd_norm_g,
    q_norm_g, k_norm_g, w_out, ln1_g, ln1_b, w_rg, b_rg, w_re, b_re, w_gate, w_up, w_down,
    ln2_g, ln2_b, norm_mix_2, w_in_2, w_pool_2, pool_scale_2, lam_re_2, lam_im_2, log_dt_2,
    b_re_2, b_im_2, c_re_2, c_im_2, d_skip_2, w_glu_2, b_glu_2, w_out_2, norm_ffn_2, w_gate_2,
    w_up_2, w_down_2, norm_final_2,
):
    x = first_block(
        x, c, ctx, c_ctx, w_mod, b_mod, w_in, conv_w, conv_b, dt_bias, a_log, d_skip,
        ssd_norm_g, q_norm_g, k_norm_g, w_out, ln1_g, ln1_b, w_rg, b_rg, w_re, b_re, w_gate,
        w_up, w_down, ln2_g, ln2_b,
    )
    return second_block(
        x, norm_mix_2, w_in_2, w_pool_2, pool_scale_2, lam_re_2, lam_im_2, log_dt_2, b_re_2,
        b_im_2, c_re_2, c_im_2, d_skip_2, w_glu_2, b_glu_2, w_out_2, norm_ffn_2, w_gate_2,
        w_up_2, w_down_2, norm_final_2,
    )


_drawn_inputs = setup_inputs


def setup_inputs(seed=0):
    import zlib

    import numpy as np

    out = dict(_drawn_inputs(seed))
    spreads = {}
    factors = {'ctx': 8.0,
     'c_ctx': 6.806,
     'b_mod': 4.61,
     'conv_b': 8.0,
     'd_skip': 200.0,
     'ssd_norm_g': 8.0,
     'q_norm_g': 8.0,
     'k_norm_g': 8.0,
     'ln1_b': 9.574,
     'b_rg': 49.357,
     'b_re': 64.0,
     'ln2_b': 20.367,
     'norm_mix_2': 6.107,
     'pool_scale_2': 6.838,
     'lam_re_2': 64.0,
     'lam_im_2': 41.408,
     'log_dt_2': 42.48,
     'b_re_2': 58.16,
     'b_im_2': 58.6,
     'c_re_2': 57.392,
     'c_im_2': 57.776,
     'b_glu_2': 200.0,
     'norm_ffn_2': 16.274,
     'norm_final_2': 22.495}
    for name, (base, spread) in spreads.items():
        noise = np.random.default_rng([zlib.crc32(name.encode()), seed]).standard_normal(out[name].shape)
        drawn = base * np.exp(spread * noise) if base else spread * noise
        out[name] = __import__('jax').numpy.asarray(drawn.astype(out[name].dtype))
    for name, factor in factors.items():
        out[name] = (out[name] * factor).astype(out[name].dtype)
    return out
```

```python
from contextlib import ExitStack

import numpy as np
import concourse.bass as bass
from concourse import mybir

F32 = mybir.dt.float32
ALU = mybir.AluOpType
ACT = mybir.ActivationFunctionType
AX = mybir.AxisListType

P = 128
D = 1024
KT = D // P
L = 1024
LT = L // P
CTX = 256
CT = CTX // P
NT = LT + CT
HALF = 512
PAN = KT * HALF

HEADS, HD = 16, 64
KVH = 4
GQA = HEADS // KVH
NST = 128
DSSD = HEADS * HD
CONVW = 5
XBC = DSSD + 2 * 2 * NST
XT = XBC // P
OFF_Q = DSSD
OFF_XBC = OFF_Q + HEADS * HD
OFF_DT = OFF_XBC + XBC
OFF_K = OFF_DT + 2 * HEADS
MODW = 6 * D
MODT = MODW // P
ALPHA = 2.0 ** 0.25
SCALE = HD ** -0.5

NE, FE = 16, 256
DFF = 2816
FB = DFF // FE
MG, EG = 4, 4

G2, SH, SP2 = 32, 16, 64
TC = P // SH
NC2 = L // TC
QG = P // SH
POOLS = (2, 4, 8, 16)
EPS_LN, EPS_RMS = 1e-5, 1e-6

RAWX, RAWC = 2, 2 + L + 4
RAW = RAWC + CTX + 2
CONV = RAW - 4

PACK = {}
_r = 0
for _n, _k in (("b_mod", MODT), ("c", KT), ("c_ctx", KT), ("conv_b", XT), ("norm_mix_2", KT),
               ("norm_ffn_2", KT), ("ssd_norm_g", KT), ("pool_scale_2", 4), ("b_glu_2", 4)):
    PACK[_n] = (_r, _k)
    _r += _k
NPACK = _r
ROWC = {}
_r = 0
for _n, _k in (("dt_bias", 32), ("a_log", 32), ("d_skip", 16), ("q_norm_g", 64), ("k_norm_g", 64),
               ("b_rg", MG), ("b_re", NE)):
    ROWC[_n] = (_r, _k)
    _r += _k
NROWC = _r


def build(nc, io, out):
    ctx = ExitStack()
    with ctx:
        def sb(name, shape, dt=F32):
            return ctx.enter_context(nc.sbuf_tensor(name, shape, dt))

        def sem(name):
            return ctx.enter_context(nc.semaphore(name))

        arena_a = sb("arena_a", [P, KT * L])
        arena_b = sb("arena_b", [P, KT * L])
        arena_c = sb("arena_c", [P, NT * DSSD])
        arena_d = sb("arena_d", [P, KT * L])
        arena_t = sb("arena_t", [P, 4096])
        ring = sb("ring", [P, 3 * PAN])
        ident = sb("ident", [P, P])
        ones = sb("ones", [P, P])
        m_le = sb("m_le", [P, P])
        m_ge = sb("m_ge", [P, P])
        m_gt = sb("m_gt", [P, P])
        m_lt = sb("m_lt", [P, P])
        cols = sb("cols", [P, NPACK])
        convw = sb("convw", [P, CONVW * XT])
        rowc = sb("rowc", [P, NROWC])
        modc = sb("modc", [P, MODT, 2])
        csil = sb("csil", [P, KT, 2])
        ps = ctx.enter_context(nc.psum_tensor("ps", [P, 8, HALF], F32))

        def view(arena, at, *shape):
            n = 1
            for s in shape:
                n *= s
            v = arena[:, at:at + n]
            if len(shape) == 1:
                return v
            names = "abcd"[:len(shape)]
            return v.rearrange("p (%s) -> p %s" % (" ".join(names), " ".join(names)),
                               **{k: s for k, s in zip(names, shape)})

        def col(name):
            at, n = PACK[name]
            return cols[:, at:at + n]

        def rowv(name):
            at, n = ROWC[name]
            return rowc[:, at:at + n]

        def bc(ap, axis, n):
            ap = ap.unsqueeze(axis)
            shape = list(ap.shape)
            shape[axis] = n
            return ap.to_broadcast(shape)

        ends = {}

        def after(eng, *stages):
            for s in stages:
                for sm, n in ends[s]:
                    eng.wait_ge(sm, n)

        def step(eng, ins, sm, n):
            ins.then_inc(sm, 1)
            eng.wait_ge(sm, n)

        class Chain:

            def __init__(self, eng, sm, n=0):
                self.eng, self.sm, self.n = eng, sm, n

            def __call__(self, ins):
                self.n += 1
                ins.then_inc(self.sm, 1)
                self.eng.wait_ge(self.sm, self.n)

        steps = sem("dve_steps")
        chained = [0]

        def panel_of(w, k0, n0):
            return w[k0:k0 + D, n0:n0 + HALF].rearrange("(k p) n -> p k n", p=P)

        w_mod, w_in, w_out = io["w_mod"][0], io["w_in"][0], io["w_out"][0]
        panels = [panel_of(w_mod, 0, HALF * n) for n in range(4)]
        J_XBC = len(panels)
        panels += [panel_of(w_in, 0, OFF_XBC + HALF * n) for n in range(3)]
        J_Z = len(panels)
        panels += [panel_of(w_in, 0, HALF * n) for n in range(2)]
        J_KV = len(panels)
        panels += [panel_of(w_in, 0, OFF_K)]
        J_Q = len(panels)
        panels += [panel_of(w_in, 0, OFF_Q + HALF * n) for n in range(2)]
        J_MOD = len(panels)
        panels += [panel_of(w_mod, 0, HALF * n) for n in range(4, 12)]
        J_OUT = len(panels)
        panels += [panel_of(w_out, D * k, HALF * n) for n in range(2) for k in range(2)]
        NPAN1 = len(panels)
        panel_in = [sem(f"panel_in{i}") for i in range(3)]
        panel_free = {}

        def slot(j):
            return view(ring, (j % 3) * PAN, KT, HALF)

        def load_panels(eng, j0, j1):
            for j in range(j0, j1):
                if j >= 3:
                    eng.wait_ge(*panel_free[j - 3])
                eng.dma_start(slot(j), panels[j]).then_inc(panel_in[j % 3], 16)

        def wait_panel(eng, j):
            eng.wait_ge(panel_in[j % 3], 16 * (j // 3 + 1))

        xin = view(arena_a, 0, LT, D)
        cin = view(arena_d, 0, CT, D)
        packa = view(arena_t, 0, P)
        packb = view(arena_t, P, P)
        hx = view(arena_b, 0, KT, L)
        hc = view(arena_t, 6 * NT * 32, KT, CTX)
        raw = [view(arena_a, i * RAW, RAW) for i in range(2)]
        cv = [view(arena_a, 2 * RAW + i * CONV, CONV) for i in range(2)]
        xs = view(arena_c, 0, NT, DSSD)
        bct = view(arena_d, 0, 4, L + CTX)
        btok = view(arena_d, 4 * (L + CTX), NT, 2 * NST)
        DT1 = NT * 32
        dts, dta, acs, eacs, cdec, wdt = (view(arena_t, i * DT1, NT, 32) for i in range(6))
        wdtw = view(arena_a, 6000, KT, 32)
        hst = view(arena_t, 6 * DT1, 2, DSSD)
        y = view(arena_a, 0, LT, DSSD)
        xw = view(arena_b, 0, 2, DSSD)
        xdt = view(arena_b, 2048, 2, DSSD)
        rr = view(arena_b, 4096, 2, HALF)
        em = view(arena_b, 5120, 2, 2, HALF)
        cbm = view(arena_b, 7168, 2, 2 * NST)
        tmp = view(arena_b, 7680, HALF)

        hx_dram = nc.dram_tensor("hx_dram", [P, KT * L], F32).ap()
        hc_dram = nc.dram_tensor("hc_dram", [P, KT * CTX], F32).ap()

        s_const = sem("constants_made")
        s_small = sem("small_loaded")
        s_x = sem("inputs_loaded")
        s_packT = sem("pack_transposed")
        s_cols = sem("columns_ready")
        s_silu = sem("conditions_ready")
        s_mod = sem("mod_product")
        s_modc = sem("mod_ready")
        s_hxT = sem("inputs_transposed")
        s_hxa, s_hxv = sem("inputs_modulated_act"), sem("inputs_modulated_dve")
        s_wdt = sem("dt_weight_loaded")
        s_dtp, s_acsp = sem("dt_product"), sem("decay_sums")
        s_dt = sem("dt_steps")
        s_dta = sem("dt_act_steps")
        s_xbc, s_rawz, s_raw, s_conv = sem("xbc_product"), sem("raw_zeroed"), sem("raw_copied"), sem("convolved")
        s_act = sem("conv_activated")
        s_xsT, s_xsc = sem("xs_transposed"), sem("xs_copied")
        s_spill = sem("hx_spilled")

        for j in range(4):
            panel_free[j] = (s_mod, j + 1)
        for j in range(3):
            panel_free[J_XBC + j] = (s_xbc, 4 * (j + 1))
        ends["hx"] = [(s_hxa, 10), (s_hxv, 14)]

        NSMALL = len(PACK) + 1 + len(ROWC)

        def sp_first(eng):
            load_panels(eng, 0, 3)
            eng.dma_start(xin, io["x"][0].rearrange("(t p) d -> p t d", p=P)).then_inc(s_x, 16)
            eng.dma_start(cin, io["ctx"][0].rearrange("(t p) d -> p t d", p=P)).then_inc(s_x, 16)
            load_panels(eng, 3, J_XBC + 3)
            after(eng, "hx")
            eng.dma_start(hx_dram, hx.rearrange("p k n -> p (k n)")).then_inc(s_spill, 16)
            eng.dma_start(hc_dram, hc.rearrange("p k n -> p (k n)")).then_inc(s_spill, 16)
            eng.dma_start(wdtw, w_in[:, OFF_DT:OFF_DT + 32].rearrange("(k p) n -> p k n", p=P)
                                  ).then_inc(s_wdt, 16)
            load_panels(eng, J_XBC + 3, J_KV)

        def act_small(eng):
            for n in PACK:
                at, k = PACK[n]
                src = io[n] if n == "c_ctx" else io[n][0]
                eng.dma_start(packa[at:at + k, :], src.rearrange("(t p) -> t p", p=P)).then_inc(s_small, 16)
            for j in range(CONVW):
                eng.dma_start(packb[j * XT:(j + 1) * XT, :],
                              io["conv_w"][0, j, :].rearrange("(t p) -> t p", p=P)).then_inc(s_small, 16)
            for n in ROWC:
                at, k = ROWC[n]
                src = io[n][0]
                if len(src.shape) == 2:
                    src = src.rearrange("a b -> (a b)")
                eng.dma_start(rowc[:, at:at + k], src.partition_broadcast(P)).then_inc(s_small, 16)

        NSMALLV = 16 * (len(PACK) + CONVW + len(ROWC))

        def pool_consts(eng):
            eng.memset(ident[:, :], 0.0).then_inc(s_const, 1)
            for m in (ones, m_le, m_ge, m_gt, m_lt):
                eng.memset(m[:, :], 1.0).then_inc(s_const, 1)
            eng.wait_ge(s_const, 6)
            eng.affine_select(out=ident[:, :], in_=ident[:, :], compare_op=ALU.not_equal, fill=1.0,
                              base=0, pattern=[[-1, P]], channel_multiplier=1).then_inc(s_const, 1)
            for m, base, cm, st in ((m_le, 0, -1, 1), (m_ge, 0, 1, -1), (m_gt, -1, 1, -1), (m_lt, -1, -1, 1)):
                eng.affine_select(out=m[:, :], in_=m[:, :], compare_op=ALU.is_ge, fill=0.0,
                                  base=base, pattern=[[st, P]], channel_multiplier=cm).then_inc(s_const, 1)

        def pe_pack(eng):
            eng.wait_ge(s_const, 11)
            eng.wait_ge(s_small, NSMALLV)
            eng.transpose(ps[:, 6, 0:NPACK], packa[0:NPACK, :], ident[0:NPACK, 0:NPACK])
            eng.transpose(ps[:, 7, 0:CONVW * XT], packb[0:CONVW * XT, :],
                          ident[0:CONVW * XT, 0:CONVW * XT]).then_inc(s_packT, 1)

        def dve_pack(eng):
            eng.wait_ge(s_packT, 1)
            eng.tensor_copy(cols[:, :], ps[:, 6, 0:NPACK])
            eng.tensor_copy(convw[:, :], ps[:, 7, 0:CONVW * XT]).then_inc(s_cols, 1)

        def act_silu_c(eng):
            eng.wait_ge(s_cols, 1)
            eng.activation(csil[:, :, 0], col("c"), ACT.Silu)
            eng.activation(csil[:, :, 1], col("c_ctx"), ACT.Silu).then_inc(s_silu, 1)

        def pe_mod(eng, part, j0, n0, n1):
            eng.wait_ge(s_silu, 1)
            for j in range(n0 // 4, n1 // 4):
                wait_panel(eng, j0 + j - n0 // 4)
                w = slot(j0 + j - n0 // 4)
                for b in range(4):
                    for k in range(KT):
                        mm = eng.matmul(ps[:, part, 2 * (4 * j + b):2 * (4 * j + b) + 2],
                                        w[:, k, b * P:(b + 1) * P], csil[:, k, :],
                                        start=(k == 0), stop=(k == KT - 1))
                mm.then_inc(s_mod, 1)

        def dve_mod(eng, part, n0, n1):
            eng.wait_ge(s_mod, n1 // 4)
            eng.wait_ge(s_cols, 1)
            src = ps[:, part, 2 * n0:2 * n1].rearrange("p (n v) -> p n v", v=2)
            eng.tensor_tensor(modc[:, n0:n1, :], src, bc(col("b_mod")[:, n0:n1], 2, 2), ALU.add
                              ).then_inc(s_modc, 1)
            k = 8 if part == 0 else 4 * KT
            eng.wait_ge(s_modc, 1 if part == 0 else 3)
            eng.tensor_scalar(modc[:, k:k + KT, :], modc[:, k:k + KT, :], 1.0, None, ALU.add
                              ).then_inc(s_modc, 1)

        HXJOBS = [(k, s, t0, n) for k in range(KT) for s, t0, n in (("x", 0, 4), ("x", 4, 4), ("c", 0, 2))]

        def hx_of(j):
            return "act" if j % 12 in (0, 2, 5, 7, 10) else "dve"

        def pe_hx(eng):
            eng.wait_ge(s_x, 32)
            for j, (k, s, t0, n) in enumerate(HXJOBS):
                if j >= 4:
                    eng.wait_ge(s_hxa, sum(hx_of(i) == "act" for i in range(j - 3)))\
                        if hx_of(j - 4) == "act" else \
                        eng.wait_ge(s_hxv, sum(hx_of(i) == "dve" for i in range(j - 3)))
                src = xin if s == "x" else cin
                for i in range(n):
                    mm = eng.transpose(ps[:, 4 + j % 4, i * P:(i + 1) * P],
                                       src[:, t0 + i, k * P:(k + 1) * P], ident[:, :])
                mm.then_inc(s_hxT, 1)

        def hx_evac(eng, who):
            eng.wait_ge(s_modc, 2)
            for j, (k, s, t0, n) in enumerate(HXJOBS):
                if hx_of(j) != who:
                    continue
                eng.wait_ge(s_hxT, j + 1)
                v = 0 if s == "x" else 1
                dst = (hx if s == "x" else hc)[:, k, t0 * P:(t0 + n) * P]
                src = ps[:, 4 + j % 4, 0:n * P]
                sc, sh = modc[:, KT + k, v:v + 1], modc[:, k, v:v + 1]
                if who == "act":
                    eng.activation(dst, src, ACT.Identity, bias=sh, scale=sc).then_inc(s_hxa, 1)
                else:
                    eng.tensor_scalar(dst, src, sc, sh, ALU.mult, ALU.add).then_inc(s_hxv, 1)

        def h_tile(k, t):
            return hx[:, k, t * P:(t + 1) * P] if t < LT else hc[:, k, (t - LT) * P:(t - LT + 1) * P]

        def pe_xbc(eng):
            after(eng, "hx")
            for m in range(XT):
                if m % 4 == 0:
                    wait_panel(eng, J_XBC + m // 4)
                w = slot(J_XBC + m // 4)
                b0 = 3 * (m % 2)
                if m >= 2:
                    eng.wait_ge(s_raw, m - 1)
                for b, src in ((b0, hx[:, :, 0:HALF]), (b0 + 1, hx[:, :, HALF:L]), (b0 + 2, hc)):
                    n = src.shape[2]
                    for k in range(KT):
                        mm = eng.matmul(ps[:, b, 0:n], w[:, k, (m % 4) * P:(m % 4 + 1) * P], src[:, k, :],
                                        start=(k == 0), stop=(k == KT - 1))
                mm.then_inc(s_xbc, 1)
                if m >= 2:
                    pe_turn(eng, m - 2)


        def pe_turn(eng, m):
            if m >= XT - 2:
                return
            eng.wait_ge(s_act, m + 1)
            for i in range(3):
                t0, t1 = ((0, 4), (4, 8), (8, 10))[i]
                u = 3 * m + i
                if u >= 2:
                    eng.wait_ge(s_xsc, u - 1)
                for t in range(t0, t1):
                    src = m_src(m)[:, t * P + (4 if t >= LT and m < 8 else 0):][:, 0:P]
                    mm = eng.transpose(ps[:, 6 + u % 2, (t - t0) * P:(t - t0 + 1) * P], src, ident[:, :])
                mm.then_inc(s_xsT, 1)

        def m_src(m):
            return cv[m % 2] if m < 8 else bct[:, m - 8, :]

        def dve_conv(eng):
            ch = Chain(eng, steps)
            after(eng, "hx")
            for r in raw:
                for a in (0, RAWX + L, RAW - 2):
                    n = 4 if a == RAWX + L else 2
                    eng.memset(r[:, a:a + n], 0.0).then_inc(s_rawz, 1)
            for m in range(XT):
                eng.wait_ge(s_raw, m + 1)
                c = cv[m % 2]
                if m >= 2:
                    eng.wait_ge(s_act, m - 1)
                    eng.wait_ge(s_xsT, 3 * (min(m, XT - 2) - 1))
                def w(j):
                    return convw[:, j * XT + m:j * XT + m + 1]
                ch(eng.tensor_scalar(c, raw[m % 2][:, 0:CONV], w(0), col("conv_b")[:, m:m + 1],
                                     ALU.mult, ALU.add))
                for j in range(1, CONVW):
                    ins = eng.scalar_tensor_tensor(out=c, in0=raw[m % 2][:, j:j + CONV], scalar=w(j), in1=c,
                                                   op0=ALU.mult, op1=ALU.add)
                    if j < CONVW - 1:
                        ch(ins)
                ins.then_inc(s_conv, 1)
            chained[0] = ch.n

        def act_xbc(eng):
            def copy_turns(m):
                if m >= XT - 2:
                    return
                for i in range(3):
                    u = 3 * m + i
                    t0, t1 = ((0, 4), (4, 8), (8, 10))[i]
                    eng.wait_ge(s_xsT, u + 1)
                    dst = (xs[:, t0:t1, m * P:(m + 1) * P] if m < 8 else
                           btok[:, t0:t1, (m - 8) * P:(m - 7) * P])
                    eng.copy(dst, ps[:, 6 + u % 2, 0:(t1 - t0) * P].rearrange("p (t c) -> p t c", c=P)
                             ).then_inc(s_xsc, 1)
            after(eng, "hx")
            eng.wait_ge(s_rawz, 6)
            for m in range(XT + 1):
                if m < XT:
                    b0 = 3 * (m % 2)
                    eng.wait_ge(s_xbc, m + 1)
                    if m >= 2:
                        eng.wait_ge(s_conv, m - 1)
                    r = raw[m % 2]
                    eng.copy(r[:, RAWX:RAWX + L], ps[:, b0:b0 + 2, :])
                    eng.copy(r[:, RAWC + 0:RAWC + CTX], ps[:, b0 + 2, 0:CTX]).then_inc(s_raw, 1)
                if m >= 1:
                    k = m - 1
                    eng.wait_ge(s_conv, k + 1)
                    if k < 8:
                        eng.activation(cv[k % 2], cv[k % 2], ACT.Silu).then_inc(s_act, 1)
                    else:
                        eng.activation(bct[:, k - 8, 0:L], cv[k % 2][:, 0:L], ACT.Silu)
                        eng.activation(bct[:, k - 8, L:L + CTX], cv[k % 2][:, L + 4:L + 4 + CTX], ACT.Silu
                                       ).then_inc(s_act, 1)
                    if k >= 1:
                        copy_turns(k - 1)

        ends["xbc"] = [(s_xbc, XT), (s_act, XT), (s_xsc, 3 * (XT - 2)), (s_xsT, 3 * (XT - 2)), (s_conv, XT)]

        def pe_dt(eng):
            after(eng, "xbc")
            eng.wait_ge(s_wdt, 16)
            for t in range(NT):
                for k in range(KT):
                    mm = eng.matmul(ps[:, 0, t * 32:(t + 1) * 32], h_tile(k, t), wdtw[:, k, :],
                                    start=(k == 0), stop=(k == KT - 1))
            mm.then_inc(s_dtp, 1)
            eng.wait_ge(s_dt, 6)
            a = dta
            eng.matmul(ps[:, 1, 0:NT * 16], m_le[:, :], a[:, :, 0:16], start=True, stop=True)
            eng.matmul(ps[:, 2, 0:NT * 16], m_ge[:, :], a[:, :, 16:32], start=True, stop=True)
            eng.matmul(ps[:, 3, 0:NT * 32], ones[:, :], a, start=True, stop=True)
            eng.matmul(ps[:, 4, 0:NT * 16], m_gt[:, :], a[:, :, 0:16], start=True, stop=True)
            eng.matmul(ps[:, 5, 0:NT * 16], m_lt[:, :], a[:, :, 16:32], start=True, stop=True
                       ).then_inc(s_acsp, 1)

        def dve_dt(eng):
            ch = Chain(eng, s_dt)
            eng.wait_ge(s_dtp, 1)
            flat = lambda v: v.rearrange("p t h -> p (t h)")
            ch(eng.tensor_tensor(acs, ps[:, 0, 0:NT * 32].rearrange("p (t h) -> p t h", h=32),
                                 bc(rowv("dt_bias"), 1, NT), ALU.add))
            ch(eng.scalar_tensor_tensor(out=flat(eacs), in0=flat(acs), scalar=-1.0, in1=flat(acs),
                                        op0=ALU.mult, op1=ALU.max))
            eng.wait_ge(s_dta, 3)
            ch(eng.scalar_tensor_tensor(out=flat(dts), in0=flat(acs), scalar=0.0, in1=flat(cdec),
                                        op0=ALU.max, op1=ALU.add))
            ch(eng.tensor_scalar(wdt[:, 0, :], wdt[:, 0, :], -1.0, None, ALU.mult))
            ch(eng.tensor_copy(eacs[:, 0, :], wdt[:, 0, :]))
            ch(eng.tensor_tensor(dta, dts, bc(eacs[:, 0, :], 1, NT), ALU.mult))
            eng.wait_ge(s_acsp, 1)
            fw = ps[:, 1, 0:NT * 16].rearrange("p (t h) -> p t h", h=16)
            bw = ps[:, 2, 0:NT * 16].rearrange("p (t h) -> p t h", h=16)
            ch(eng.tensor_copy(acs[:, :, 0:16], fw))
            ch(eng.tensor_copy(acs[:, :, 16:32], bw))
            eng.wait_ge(s_dta, 7)
            ch(eng.tensor_tensor(wdt, wdt, dts, ALU.mult))

        def act_dt(eng):
            eng.wait_ge(s_dt, 2)
            eng.wait_ge(s_small, NSMALLV)
            flat = lambda v: v.rearrange("p t h -> p (t h)")
            eng.activation(flat(cdec), flat(eacs), ACT.Exp, scale=-1.0).then_inc(s_dta, 1)
            eng.activation(wdt[:, 0, :], rowv("a_log"), ACT.Exp).then_inc(s_dta, 1)
            eng.wait_ge(s_dta, 1)
            eng.activation(flat(cdec), flat(cdec), ACT.Ln, bias=1.0).then_inc(s_dta, 1)
            eng.wait_ge(s_acsp, 1)
            eng.activation(wdt[:, :, 0:16], ps[:, 4, 0:NT * 16].rearrange("p (t h) -> p t h", h=16), ACT.Exp
                           ).then_inc(s_dta, 1)
            eng.activation(wdt[:, :, 16:32], ps[:, 5, 0:NT * 16].rearrange("p (t h) -> p t h", h=16), ACT.Exp
                           ).then_inc(s_dta, 1)
            eng.activation(flat(cdec), ps[:, 3, 0:NT * 32], ACT.Exp).then_inc(s_dta, 1)
            eng.wait_ge(s_dt, 8)
            eng.activation(flat(eacs), flat(acs), ACT.Exp).then_inc(s_dta, 1)

        ends["dt"] = [(s_dt, 9), (s_dta, 7)]

        
        s_xw, s_xdt = sem("state_inputs_scaled"), sem("diagonal_inputs_scaled")
        s_yoff, s_st = sem("carried_products"), sem("state_products")
        s_yoffd, s_h = sem("carried_added"), sem("states_updated")
        s_cb, s_cbm = sem("cb_product"), sem("cb_masked")
        s_rr, s_diff, s_exp = sem("decay_terms"), sem("decay_differences"), sem("decays")
        s_m, s_dg, s_dgd = sem("mixing_ready"), sem("diagonal_product"), sem("diagonal_added")
        STEPS = [((LT + n, NT - 1 - n) if n < CT else (n - CT, NT - 1 - n)) for n in range(NT)]
        SSD_LATENT = range(CT, NT)

        def dve_ssd(eng):
            ch = Chain(eng, steps, chained[0])
            after(eng, "xbc", "dt")
            eng.wait_ge(s_spill, 32)
            ch(eng.memset(hst, 0.0))
            for t in range(LT):
                ch(eng.tensor_tensor(y[:, t, :].rearrange("p (h c) -> p h c", c=HD),
                                     xs[:, t, :].rearrange("p (h c) -> p h c", c=HD),
                                     bc(rowv("d_skip"), 2, HD), ALU.mult))

            def scaled(dst, t, d, w):
                return eng.tensor_tensor(dst[:, d, :].rearrange("p (h c) -> p h c", c=HD),
                                         xs[:, t, :].rearrange("p (h c) -> p h c", c=HD),
                                         bc(w[:, t, 16 * d:16 * d + 16], 2, HD), ALU.mult)

            for n, pair in enumerate(STEPS):
                if n >= 1:
                    eng.wait_ge(s_st, 4 * n)
                for d in range(2):
                    scaled(xw, pair[d], d, wdt).then_inc(s_xw, 1)
                for d, t in enumerate(pair):
                    for g in range(2):
                        cs = slice(g * HALF, (g + 1) * HALF)
                        if n >= CT:
                            eng.wait_ge(s_yoff, 4 * (n - CT) + 2 * d + g + 1)
                            step(eng, eng.tensor_tensor(
                                tmp.rearrange("p (h c) -> p h c", c=HD),
                                ps[:, 2 + g, :].rearrange("p (h c) -> p h c", c=HD),
                                bc(eacs[:, t, 16 * d + 8 * g:16 * d + 8 * g + 8], 2, HD), ALU.mult),
                                s_yoffd, 4 * (n - CT) + 2 * d + g + 1)
                            ch(eng.tensor_tensor(y[:, t, cs], y[:, t, cs], tmp, ALU.add))
                        eng.wait_ge(s_st, 4 * n + 2 * d + g + 1)
                        h3 = hst[:, d, cs].rearrange("p (h c) -> p h c", c=HD)
                        ch(eng.tensor_tensor(h3, h3, bc(cdec[:, t, 16 * d + 8 * g:16 * d + 8 * g + 8], 2, HD),
                                             ALU.mult))
                        step(eng, eng.tensor_tensor(hst[:, d, cs], hst[:, d, cs], ps[:, 4 + g, :], ALU.add),
                             s_h, 4 * n + 2 * d + g + 1)
                if n < CT:
                    continue
                c = pair[0]
                if c >= 1:
                    eng.wait_ge(s_dg, 4 * c)
                for d in range(2):
                    scaled(xdt, c, d, dts).then_inc(s_xdt, 1)
                eng.wait_ge(s_cb, c + 1)
                eng.tensor_tensor(cbm[:, 0, :].rearrange("p (g q) -> p g q", g=2),
                                  ps[:, 0, 0:2 * P].rearrange("p (g q) -> p g q", g=2),
                                  bc(m_le[:, :], 1, 2), ALU.mult)
                eng.tensor_tensor(cbm[:, 1, :].rearrange("p (g q) -> p g q", g=2),
                                  ps[:, 0, 0:2 * P].rearrange("p (g q) -> p g q", g=2),
                                  bc(m_ge[:, :], 1, 2), ALU.mult).then_inc(s_cbm, 1)
                eng.wait_ge(s_cbm, c + 1)
                for hb in range(4):
                    k = 4 * c + hb
                    g = hb // 2
                    eng.wait_ge(s_exp, k + 1)
                    for d in range(2):
                        e3 = em[:, k % 2, d, :].rearrange("p (h q) -> p h q", h=4)
                        ins = eng.tensor_tensor(e3, e3, bc(cbm[:, d, g * P:(g + 1) * P], 1, 4), ALU.mult)
                    ins.then_inc(s_m, 1)
                    if hb % 2 == 1:
                        eng.wait_ge(s_dg, k + 1)
                        cs = slice(g * HALF, (g + 1) * HALF)
                        step(eng, eng.tensor_tensor(y[:, c, cs], y[:, c, cs], ps[:, 1, :], ALU.add),
                             s_dgd, 2 * c + g + 1)

            chained[0] = ch.n

        def pool_ssd(eng):
            after(eng, "xbc", "dt")
            eng.wait_ge(s_spill, 32)
            for k in range(4 * LT):
                c, hb = k // 4, k % 4
                if k >= 1:
                    eng.wait_ge(s_diff, k)
                for d, m in enumerate((m_le, m_ge)):
                    ins = eng.tensor_tensor(rr[:, d, :].rearrange("p (h q) -> p h q", h=4),
                                            bc(m[:, :], 1, 4),
                                            bc(dta[:, c, 16 * d + 4 * hb:16 * d + 4 * hb + 4], 2, P),
                                            ALU.mult)
                ins.then_inc(s_rr, 1)

        def act_ssd(eng):
            for k in range(4 * LT):
                eng.wait_ge(s_diff, k + 1)
                if k >= 2:
                    eng.wait_ge(s_dg, k - 1)
                for d in range(2):
                    ins = eng.activation(em[:, k % 2, d, :], ps[:, 6 + d, :], ACT.Exp)
                ins.then_inc(s_exp, 1)

        def pe_ssd(eng):
            def tcols(t):
                return slice(t * P, (t + 1) * P)

            def diff(k):
                eng.wait_ge(s_rr, k + 1)
                if k >= 1:
                    eng.wait_ge(s_exp, k)
                eng.matmul(ps[:, 6, :], m_gt[:, :], rr[:, 0, :], start=True, stop=True)
                eng.matmul(ps[:, 7, :], m_lt[:, :], rr[:, 1, :], start=True, stop=True).then_inc(s_diff, 1)

            def diag(k):
                c, hb = k // 4, k % 4
                eng.wait_ge(s_m, k + 1)
                if k % 2 == 0 and k >= 2:
                    eng.wait_ge(s_dgd, k // 2)
                for h in range(4):
                    hd = 4 * hb + h
                    for d in range(2):
                        mm = eng.matmul(ps[:, 1, (hd % 8) * HD:(hd % 8 + 1) * HD],
                                        em[:, k % 2, d, h * P:(h + 1) * P],
                                        xdt[:, d, hd * HD:(hd + 1) * HD], start=(d == 0), stop=(d == 1))
                mm.then_inc(s_dg, 1)

            after(eng, "dt")
            for n, pair in enumerate(STEPS):
                for d, t in enumerate(pair):
                    for g in range(2):
                        cs = slice(g * HALF, (g + 1) * HALF)
                        if n >= CT:
                            eng.wait_ge(s_h, 4 * (n - 1) + 2 * d + g + 1)
                            j = 4 * (n - CT) + 2 * d + g
                            if j >= 2:
                                eng.wait_ge(s_yoffd, j - 1)
                            eng.matmul(ps[:, 2 + g, :], bct[:, 2 + g, tcols(t)], hst[:, d, cs],
                                       start=True, stop=True).then_inc(s_yoff, 1)
                        eng.wait_ge(s_xw, 2 * n + d + 1)
                        j = 4 * n + 2 * d + g
                        if j >= 2:
                            eng.wait_ge(s_h, j - 1)
                        eng.matmul(ps[:, 4 + g, :], btok[:, t, g * P:(g + 1) * P], xw[:, d, cs],
                                   start=True, stop=True).then_inc(s_st, 1)
                if n < CT:
                    continue
                c = pair[0]
                if c >= 1:
                    eng.wait_ge(s_cbm, c)
                for g in range(2):
                    mm = eng.matmul(ps[:, 0, g * P:(g + 1) * P], bct[:, g, tcols(c)], bct[:, 2 + g, tcols(c)],
                                    start=True, stop=True)
                mm.then_inc(s_cb, 1)
                if c == 0:
                    diff(0)
                eng.wait_ge(s_xdt, 2 * c + 2)
                for hb in range(4):
                    k = 4 * c + hb
                    if k + 1 < 4 * LT:
                        diff(k + 1)
                    diag(k)

        N_SSD_SV = (CONVW - 1) * XT + 1 + LT + LT * 4 + NT * 4
        ends["ssd"] = [(steps, N_SSD_SV), (s_h, 4 * NT), (s_dgd, 2 * LT), (s_m, 4 * LT), (s_dg, 4 * LT),
                       (s_exp, 4 * LT), (s_rr, 4 * LT)]

        mixl = view(arena_c, 0, KT, L)
        zs = [view(arena_d, i * DSSD, DSSD) for i in range(2)]
        sqz = view(arena_d, 2 * DSSD, HALF)
        ssum = view(arena_d, 3 * DSSD, 2 * LT)
        rst = view(arena_d, 3 * DSSD + 16, 2 * LT)
        ropes = sb("ropes", [P, 2, LT, HD // 2])
        s_rope = sem("rope_loaded")
        s_hxb = sem("hx_reloaded")
        s_z, s_zs, s_zg, s_zss = sem("z_product"), sem("z_activated"), sem("gated"), sem("gate_squares")
        s_zr, s_zn, s_zq = sem("gate_roots"), sem("gate_normed"), sem("gate_steps")
        s_zT, s_zTc = sem("gate_transposed"), sem("gate_copied")

        panel_free[J_Z] = panel_free[J_Z + 1] = (s_z, 2 * LT)

        def sp_gate(eng):
            for a in range(2):
                eng.dma_start(ropes[:, a], io["rope_table"][a].rearrange("(t p) c -> p t c", p=P)
                              ).then_inc(s_rope, 16)
            after(eng, "ssd")
            eng.dma_start(hx.rearrange("p k n -> p (k n)"), hx_dram).then_inc(s_hxb, 16)
            eng.dma_start(hc.rearrange("p k n -> p (k n)"), hc_dram).then_inc(s_hxb, 16)
            load_panels(eng, J_KV, NPAN1 - 1)

        def pe_gate(eng):
            after(eng, "ssd")
            eng.wait_ge(s_hxb, 32)
            wait_panel(eng, J_Z)
            wait_panel(eng, J_Z + 1)
            for t in range(LT):
                for n in range(2):
                    if t >= 2:
                        eng.wait_ge(s_zs, 2 * (t - 2) + n + 1)
                    for k in range(KT):
                        mm = eng.matmul(ps[:, 2 * (t % 2) + n, :], h_tile(k, t), slot(J_Z + n)[:, k, :],
                                        start=(k == 0), stop=(k == KT - 1))
                    mm.then_inc(s_z, 1)
            eng.wait_ge(s_zn, 2 * LT)
            for t in range(LT):
                for q in range(2):
                    u = 2 * t + q
                    if u >= 4:
                        eng.wait_ge(s_zTc, u - 3)
                    for i in range(4):
                        mm = eng.transpose(ps[:, 4 + u % 4, i * P:(i + 1) * P],
                                           y[:, t, (4 * q + i) * P:(4 * q + i + 1) * P], ident[:, :])
                    mm.then_inc(s_zT, 1)

        def act_gate(eng):
            after(eng, "ssd")
            for t in range(LT):
                if t >= 2:
                    eng.wait_ge(s_zg, 2 * (t - 1))
                for n in range(2):
                    eng.wait_ge(s_z, 2 * t + n + 1)
                    eng.activation(zs[t % 2][:, n * HALF:(n + 1) * HALF], ps[:, 2 * (t % 2) + n, :], ACT.Silu
                                   ).then_inc(s_zs, 1)
                if t >= 1:
                    gate_squares(eng, t - 1)
            gate_squares(eng, LT - 1)
            eng.wait_ge(s_zq, 1)
            eng.activation(rst, ssum, ACT.Sqrt).then_inc(s_zr, 1)

        def gate_squares(eng, t):
            for n in range(2):
                u = 2 * t + n
                eng.wait_ge(s_zg, u + 1)
                if u >= 1:
                    eng.wait_ge(s_zss, u)
                eng.activation(sqz, y[:, t, n * HALF:(n + 1) * HALF], ACT.Square,
                               accum_out=ssum[:, u:u + 1]).then_inc(s_zss, 1)

        def dve_gate(eng):
            for t in range(LT):
                for n in range(2):
                    cs = slice(n * HALF, (n + 1) * HALF)
                    eng.wait_ge(s_zs, 2 * t + n + 1)
                    eng.tensor_tensor(y[:, t, cs], y[:, t, cs], zs[t % 2][:, cs], ALU.mult).then_inc(s_zg, 1)
            ch = Chain(eng, s_zq)
            eng.wait_ge(s_zss, 2 * LT)
            ch(eng.tensor_scalar(ssum, ssum, 1.0 / HALF, EPS_RMS, ALU.mult, ALU.add))
            eng.wait_ge(s_zr, 1)
            ch(eng.reciprocal(rst, rst))
            for t in range(LT):
                for n in range(2):
                    cs = slice(n * HALF, (n + 1) * HALF)
                    eng.tensor_scalar(y[:, t, cs], y[:, t, cs], rst[:, 2 * t + n:2 * t + n + 1], None, ALU.mult
                                      ).then_inc(s_zn, 1)
            for t in range(LT):
                for q in range(2):
                    u = 2 * t + q
                    eng.wait_ge(s_zT, u + 1)
                    eng.tensor_tensor(mixl[:, 4 * q:4 * q + 4, t * P:(t + 1) * P],
                                      ps[:, 4 + u % 4, :].rearrange("p (k n) -> p k n", k=4),
                                      bc(col("ssd_norm_g")[:, 4 * q:4 * q + 4], 2, P), ALU.mult
                                      ).then_inc(s_zTc, 1)

        ends["gate"] = [(s_zTc, 2 * LT), (s_zq, 2), (s_zs, 2 * LT), (s_zss, 2 * LT), (s_zr, 1)]

        kT = view(arena_d, 0, KVH, L + CTX)
        vv = view(arena_d, 5120, NT, KVH * HD)
        qT = view(arena_a, 0, KT, L)
        mixu = qT
        qss = sb("qss", [P, 2, 2, HEADS])
        rsq = view(arena_t, 0, DSSD)
        rqn = {256: view(arena_t, 1024, 256), 1024: view(arena_t, 1024, 1024)}
        rt = {256: view(arena_t, 1280, 2, P), 1024: view(arena_t, 2048, 2, HALF)}
        rkr = view(arena_t, 1536, 256)
        rqr = [view(arena_c, 8192 + i * DSSD, DSSD) for i in range(2)]
        s_qg = sem("q_gain_scaled")
        s_qkp, s_qks, s_qkv = sem("qkv_product"), sem("qkv_squares"), sem("v_copied")
        s_qkm, s_qkr = sem("qkv_means"), sem("qkv_roots")
        s_qkn = sem("qkv_rotated")
        s_qkT, s_qkTc = sem("qkv_transposed"), sem("qkv_copied")
        JOBS = [("k", t) for t in range(NT)] + [("q", t) for t in range(LT)]
        NJ = len(JOBS)
        panel_free[J_KV] = (s_qkp, NT)
        panel_free[J_Q] = panel_free[J_Q + 1] = (s_qkp, NJ)

        def pe_qkv(eng):
            after(eng, "gate")
            wait_panel(eng, J_KV)
            for j in range(NJ + 2):
                if j < NJ:
                    kind, t = JOBS[j]
                    if j == NT:
                        wait_panel(eng, J_Q)
                        wait_panel(eng, J_Q + 1)
                    if j >= 2:
                        eng.wait_ge(s_qkn, j - 1)
                        eng.wait_ge(s_qkv, min(j - 1, NT))
                    for n in range(2 if kind == "q" else 1):
                        w = slot(J_Q + n) if kind == "q" else slot(J_KV)
                        for k in range(KT):
                            mm = eng.matmul(ps[:, 2 * (j % 2) + n, :], h_tile(k, t), w[:, k, :],
                                            start=(k == 0), stop=(k == KT - 1))
                    mm.then_inc(s_qkp, 1)
                if j >= 2:
                    i = j - 2
                    kind, t = JOBS[i]
                    eng.wait_ge(s_qkn, i + 1)
                    if i >= 2:
                        eng.wait_ge(s_qkTc, i - 1)
                    for b in range(4 if kind == "k" else 8):
                        mm = eng.transpose(ps[:, 4 + 2 * (i % 2) + b // 4, (b % 4) * P:(b % 4 + 1) * P],
                                           rqr[i % 2][:, b * P:(b + 1) * P], ident[:, :])
                    mm.then_inc(s_qkT, 1)

        def act_qkv(eng):
            after(eng, "gate")
            for j in range(NJ + 2):
                if j < NJ:
                    kind, t = JOBS[j]
                    n = 1024 if kind == "q" else 256
                    src = ps[:, 2 * (j % 2):2 * (j % 2) + 2, :].rearrange("p a b -> p (a b)")
                    eng.wait_ge(s_qkp, j + 1)
                    if j >= 1:
                        eng.wait_ge(s_qkm, 2 * j)
                    eng.activation(rsq[:, 0:n], src[:, 0:n], ACT.Square).then_inc(s_qks, 1)
                    if kind == "k":
                        eng.copy(vv[:, t, :], src[:, 256:512]).then_inc(s_qkv, 1)
                    nh = n // HD
                    eng.wait_ge(s_qkm, 2 * j + 2)
                    eng.activation(qss[:, j % 2, 1, 0:nh], qss[:, j % 2, 0, 0:nh], ACT.Sqrt).then_inc(s_qkr, 1)
                if j >= 2:
                    i = j - 2
                    kind, t = JOBS[i]
                    eng.wait_ge(s_qkT, i + 1)
                    src = ps[:, 4 + 2 * (i % 2):6 + 2 * (i % 2), :].rearrange("p a (b n) -> p (a b) n", n=P)
                    if kind == "k":
                        eng.copy(kT[:, :, t * P:(t + 1) * P], src[:, 0:4, :]).then_inc(s_qkTc, 1)
                    else:
                        eng.copy(qT[:, :, t * P:(t + 1) * P], src).then_inc(s_qkTc, 1)

        def dve_qkv(eng):
            ch = Chain(eng, steps, chained[0])
            after(eng, "gate")
            eng.wait_ge(s_rope, 32)
            step(eng, eng.tensor_scalar(rowv("q_norm_g"), rowv("q_norm_g"), SCALE, None, ALU.mult), s_qg, 1)
            for j in range(NJ + 1):
                if j < NJ:
                    kind, t = JOBS[j]
                    nh = HEADS if kind == "q" else KVH
                    eng.wait_ge(s_qks, j + 1)
                    m = qss[:, j % 2, 0, 0:nh]
                    step(eng, eng.tensor_reduce(m, rsq[:, 0:nh * HD].rearrange("p (h c) -> p h c", c=HD),
                                                AX.X, ALU.add), s_qkm, 2 * j + 1)
                    eng.tensor_scalar(m, m, 1.0 / HD, EPS_RMS, ALU.mult, ALU.add).then_inc(s_qkm, 1)
                if j >= 1:
                    i = j - 1
                    kind, t = JOBS[i]
                    nh = HEADS if kind == "q" else KVH
                    n = nh * HD
                    r = qss[:, i % 2, 1, 0:nh]
                    eng.wait_ge(s_qkr, i + 1)
                    ch(eng.reciprocal(r, r))
                    src = ps[:, 2 * (i % 2):2 * (i % 2) + 2, :].rearrange("p a (h c) -> p (a h) c", c=HD)
                    qn = rqn[n].rearrange("p (h c) -> p h c", c=HD)
                    g = rowv("q_norm_g" if kind == "q" else "k_norm_g")
                    ch(eng.tensor_tensor(qn, src[:, 0:nh, :], bc(r, 2, HD), ALU.mult))
                    ch(eng.tensor_tensor(qn, qn, bc(g, 1, nh), ALU.mult))
                    if i >= 2:
                        eng.wait_ge(s_qkT, i - 1)
                    o = rqr[i % 2][:, 0:n] if kind == "q" else rkr
                    if t < LT:
                        x2 = rqn[n].rearrange("p (h c e) -> p h c e", c=HD // 2, e=2)
                        o2 = o.rearrange("p (h c e) -> p h c e", c=HD // 2, e=2)
                        ta = rt[n][:, 0, :].rearrange("p (h c) -> p h c", c=HD // 2)
                        tb = rt[n][:, 1, :].rearrange("p (h c) -> p h c", c=HD // 2)
                        cs, sn = (bc(ropes[:, a, t, :], 1, nh) for a in range(2))
                        eng.tensor_tensor(ta, x2[:, :, :, 0], cs, ALU.mult)
                        ch(eng.tensor_tensor(tb, x2[:, :, :, 1], sn, ALU.mult))
                        ch(eng.tensor_tensor(o2[:, :, :, 0], ta, tb, ALU.subtract))
                        eng.tensor_tensor(ta, x2[:, :, :, 0], sn, ALU.mult)
                        ch(eng.tensor_tensor(tb, x2[:, :, :, 1], cs, ALU.mult))
                        ins = eng.tensor_tensor(o2[:, :, :, 1], ta, tb, ALU.add)
                        if kind == "k":
                            ch(ins)
                    if kind == "k":
                        o3 = (rkr if t < LT else rqn[n]).rearrange("p (h c) -> p h c", c=HD)
                        dup = rqr[i % 2][:, 0:2 * n].rearrange("p (h a c) -> p h a c", a=2, c=HD)
                        ins = eng.tensor_copy(dup, bc(o3, 2, 2))
                    ins.then_inc(s_qkn, 1)
            chained[0] = ch.n

        ends["qkv"] = [(s_qkn, NJ), (s_qkT, NJ), (s_qkTc, NJ), (s_qkv, NT)]

        for j in range(8):
            panel_free[J_MOD + j] = (s_mod, 4 + j + 1)

        s_wo = sem("out_product")
        for j in range(4):
            panel_free[J_OUT + j] = (s_wo, LT * (j // 2 + 1))

        def pe_mod2(eng):
            after(eng, "qkv")
            pe_mod(eng, 1, J_MOD, 16, MODT)

        def dve_mod2(eng):
            dve_mod(eng, 1, 16, MODT)

        ends["mod2"] = [(s_mod, 12), (s_modc, 4)]

        NK = L + CTX
        NAT = LT * HEADS
        pex = [view(arena_b, i * NK, NK) for i in range(2)]
        pT = [view(arena_b, (2 + i) * NK, NT, P) for i in range(2)]
        ao = [view(arena_b, 4 * NK + i * DSSD, DSSD) for i in range(2)]
        amx = view(arena_b, 4 * NK + 2 * DSSD, 2)
        asm = view(arena_b, 4 * NK + 2 * DSSD + 2, 2)
        ari = view(arena_b, 4 * NK + 2 * DSSD + 4, 2)
        s_S, s_mx, s_ex = sem("scores"), sem("score_max"), sem("exponentials")
        s_pt = sem("probs_transposed")
        s_pca, s_pcv = sem("probs_copied_act"), sem("probs_copied_dve")
        s_pv, s_ri, s_o = sem("pv_product"), sem("sum_inverted"), sem("output_scaled")
        s_oT, s_oTc = sem("output_transposed"), sem("output_copied")
        GRP = ((0, 4), (4, 8), (8, 10))

        def pe_att(eng):
            after(eng, "qkv", "mod2")

            def scores(it):
                t, h = it // HEADS, it % HEADS
                half = slice(HD * (h % 2), HD * (h % 2) + HD)
                b0 = 3 * (it % 2)
                if it >= 2:
                    eng.wait_ge(s_pca, it - 1)
                    eng.wait_ge(s_pcv, 2 * (it - 1))
                for b, (k0, k1) in enumerate(((0, HALF), (HALF, L), (L, NK))):
                    mm = eng.matmul(ps[:, b0 + b, 0:k1 - k0], qT[half, h // 2, t * P:(t + 1) * P],
                                    kT[half, h // GQA, k0:k1], start=True, stop=True)
                mm.then_inc(s_S, 1)

            def turn(it):
                b0 = 3 * (it % 2)
                eng.wait_ge(s_ex, it + 1)
                for i, (a, b) in enumerate(GRP):
                    for k in range(a, b):
                        mm = eng.transpose(ps[:, b0 + i, (k - a) * P:(k - a + 1) * P],
                                           pex[it % 2][:, k * P:(k + 1) * P], ident[:, :])
                    mm.then_inc(s_pt, 1)

            def pv(it):
                h = it % HEADS
                eng.wait_ge(s_pca, it + 1)
                eng.wait_ge(s_pcv, 2 * (it + 1))
                if it >= 2:
                    eng.wait_ge(s_o, it - 1)
                kv = h // GQA
                for k in range(NT):
                    mm = eng.matmul(ps[:, 6 + it % 2, 0:HD], pT[it % 2][:, k, :],
                                    vv[:, k, kv * HD:(kv + 1) * HD], start=(k == 0), stop=(k == NT - 1))
                mm.then_inc(s_pv, 1)

            def out_turn(t):
                eng.wait_ge(s_o, HEADS * (t + 1))
                for i in range(8):
                    mm = eng.transpose(ps[:, 6 + i // 4, (i % 4) * P:(i % 4 + 1) * P],
                                       ao[t % 2][:, i * P:(i + 1) * P], ident[:, :])
                mm.then_inc(s_oT, 1)

            scores(0)
            scores(1)
            for it in range(NAT):
                turn(it)
                if it >= 1:
                    if it >= 2 and (it - 1) % HEADS == 0:
                        out_turn((it - 1) // HEADS - 1)
                        eng.wait_ge(s_oTc, (it - 1) // HEADS)
                    pv(it - 1)
                if it + 2 < NAT:
                    scores(it + 2)
            pv(NAT - 1)
            out_turn(LT - 1)

        def act_att(eng):
            after(eng, "qkv")
            def exps(it):
                eng.wait_ge(s_mx, it + 1)
                if it >= 2:
                    eng.wait_ge(s_pt, 3 * (it - 1))
                    eng.wait_ge(s_ri, it - 1)
                s = ps[:, 3 * (it % 2):3 * (it % 2) + 3, :].rearrange("p a b -> p (a b)")
                eng.activation(pex[it % 2], s[:, 0:NK], ACT.Exp, bias=amx[:, it % 2:it % 2 + 1],
                               accum_out=asm[:, it % 2:it % 2 + 1]).then_inc(s_ex, 1)

            exps(0)
            exps(1)
            for it in range(NAT):
                eng.wait_ge(s_pt, 3 * it + 2)
                eng.copy(pT[it % 2][:, 4:8, :].rearrange("p a b -> p (a b)"), ps[:, 3 * (it % 2) + 1, :]
                         ).then_inc(s_pca, 1)
                if it + 2 < NAT:
                    exps(it + 2)

        def dve_att(eng):
            after(eng, "qkv")

            def maxi(it):
                eng.wait_ge(s_S, it + 1)
                s = ps[:, 3 * (it % 2):3 * (it % 2) + 3, :].rearrange("p a b -> p (a b)")
                if it >= 2:
                    eng.wait_ge(s_ex, it - 1)
                eng.tensor_reduce(amx[:, it % 2:it % 2 + 1], s[:, 0:NK], AX.X, ALU.max, negate=True
                                  ).then_inc(s_mx, 1)

            def scale(it):
                t, h = it // HEADS, it % HEADS
                eng.wait_ge(s_ex, it + 1)
                step(eng, eng.reciprocal(ari[:, it % 2:it % 2 + 1], asm[:, it % 2:it % 2 + 1]), s_ri, it + 1)
                eng.wait_ge(s_pv, it + 1)
                eng.tensor_scalar(ao[t % 2][:, h * HD:(h + 1) * HD], ps[:, 6 + it % 2, 0:HD],
                                  ari[:, it % 2:it % 2 + 1], None, ALU.mult).then_inc(s_o, 1)

            def out_copy(t):
                eng.wait_ge(s_oT, t + 1)
                eng.tensor_copy(mixu[:, :, t * P:(t + 1) * P],
                                ps[:, 6:8, :].rearrange("p a (b n) -> p (a b) n", n=P)).then_inc(s_oTc, 1)

            maxi(0)
            maxi(1)
            for it in range(NAT):
                for i, (a, b) in ((0, GRP[0]), (2, GRP[2])):
                    eng.wait_ge(s_pt, 3 * it + i + 1)
                    eng.tensor_copy(pT[it % 2][:, a:b, :].rearrange("p a b -> p (a b)"),
                                    ps[:, 3 * (it % 2) + i, 0:(b - a) * P]).then_inc(s_pcv, 1)
                if it >= 1:
                    if it >= 2 and (it - 1) % HEADS == 0:
                        out_copy((it - 1) // HEADS - 1)
                    scale(it - 1)
                if it + 2 < NAT:
                    maxi(it + 2)
            scale(NAT - 1)
            out_copy(LT - 1)

        ends["att"] = [(s_oTc, LT), (s_pv, NAT), (s_pca, NAT), (s_ex, NAT)]

        x1 = view(arena_b, 0, LT, D)
        xl = [view(arena_d, i * HALF, HALF) for i in range(4)]
        rowg = view(arena_d, 4096, D)
        lng, lnb = view(arena_d, 5120, D), view(arena_d, 6144, D)
        wr = view(arena_d, 7168, KT, MG + NE)
        bst = view(arena_d, 7400, LT, 2, 6)
        mv = view(arena_d, 7500, LT, 2)
        rs8 = view(arena_d, 7520, LT)
        s_ln = sem("norm_rows_loaded")
        s_rg, s_rgc = sem("gate_row_product"), sem("gate_row_copied")
        s_xl, s_wod = [sem(f"input_piece_loaded{i}") for i in range(4)], sem("out_added")
        s_lv, s_la = sem("norm_steps"), sem("norm_roots")
        N_LV = 4 + 2 * LT
        s_l1 = sem("normed")
        s_wr = sem("router_weights_loaded")

        def sp_out(eng):
            after(eng, "att")
            eng.dma_start(lng, io["ln1_g"][0].partition_broadcast(P)).then_inc(s_ln, 16)
            eng.dma_start(lnb, io["ln1_b"][0].partition_broadcast(P)).then_inc(s_ln, 16)
            eng.dma_start(wr[:, :, 0:MG], io["w_rg"][0].rearrange("(k p) n -> p k n", p=P)).then_inc(s_wr, 16)
            eng.dma_start(wr[:, :, MG:], io["w_re"][0].rearrange("(k p) n -> p k n", p=P)).then_inc(s_wr, 16)
            for u in range(2 * LT):
                n, t = u // LT, u % LT
                if u == 9:
                    load_panels(eng, NPAN1 - 1, NPAN1)
                if u >= 4:
                    eng.wait_ge(s_wod, u - 3)
                eng.dma_start(xl[u % 4], io["x"][0, t * P:(t + 1) * P, n * HALF:(n + 1) * HALF]
                              ).then_inc(s_xl[u % 4], 16)

        def pe_row(eng, piece, i):
            for k in range(KT):
                mm = eng.matmul(ps[:, 6 + k // 4, (k % 4) * P:(k % 4 + 1) * P],
                                modc[:, piece * KT + k, 0:1].to_broadcast([P, P]), ident[:, :],
                                start=True, stop=True)
            mm.then_inc(s_rg, 1)

        def pe_out(eng):
            after(eng, "att", "mod2")
            pe_row(eng, 2, 0)
            for n in range(2):
                wait_panel(eng, J_OUT + 2 * n)
                wait_panel(eng, J_OUT + 2 * n + 1)
                for t in range(LT):
                    u = n * LT + t
                    if u >= 4:
                        eng.wait_ge(s_wod, u - 3)
                    for k in range(2 * KT):
                        src = mixl if k < KT else mixu
                        mm = eng.matmul(ps[:, u % 4, :], src[:, k % KT, t * P:(t + 1) * P],
                                        slot(J_OUT + 2 * n + k // KT)[:, k % KT, :],
                                        start=(k == 0), stop=(k == 2 * KT - 1))
                    mm.then_inc(s_wo, 1)

        def row_copy(eng, i):
            eng.wait_ge(s_rg, i + 1)
            step(eng, eng.tensor_copy(rowg, ps[:, 6:8, :].rearrange("p a n -> p (a n)")), s_rgc, i + 1)

        def dve_norm(eng, i):
            ch = Chain(eng, s_lv, N_LV * i)
            for t in range(LT):
                for n in range(2):
                    ins = eng.bn_stats(bst[:, t, n, :], x1[:, t, n * HALF:(n + 1) * HALF])
            ch(ins)
            for t in range(LT):
                ins = eng.bn_aggr(mv[:, t, :], bst[:, t, :, :].rearrange("p a b -> p (a b)"))
            ch(ins)
            ch(eng.tensor_scalar(mv[:, :, 1], mv[:, :, 1], EPS_LN, None, ALU.add))
            eng.wait_ge(s_la, i + 1)
            ch(eng.reciprocal(rs8, rs8))
            eng.wait_ge(s_ln, 32 * (i + 1))
            for t in range(LT):
                ch(eng.tensor_scalar(x1[:, t, :], x1[:, t, :], mv[:, t, 0:1], rs8[:, t:t + 1],
                                     ALU.subtract, ALU.mult))
                ch(eng.tensor_tensor(x1[:, t, :], x1[:, t, :], lng, ALU.mult))
                step(eng, eng.tensor_tensor(x1[:, t, :], x1[:, t, :], lnb, ALU.add), s_l1, LT * i + t + 1)

        def act_norm(eng, i):
            eng.wait_ge(s_lv, N_LV * i + 3)
            eng.activation(rs8, mv[:, :, 1], ACT.Sqrt).then_inc(s_la, 1)

        def dve_out(eng):
            row_copy(eng, 0)
            for u in range(2 * LT):
                n, t = u // LT, u % LT
                cs = slice(n * HALF, (n + 1) * HALF)
                eng.wait_ge(s_wo, u + 1)
                if u == 0:
                    after(eng, "att")
                ins = eng.tensor_tensor(x1[:, t, cs], ps[:, u % 4, :], rowg[:, cs], ALU.mult)
                step(eng, ins, s_wot, u + 1)
                eng.wait_ge(s_xl[u % 4], 16 * (u // 4 + 1))
                step(eng, eng.scalar_tensor_tensor(out=x1[:, t, cs], in0=xl[u % 4], scalar=ALPHA,
                                                   in1=x1[:, t, cs], op0=ALU.mult, op1=ALU.add),
                     s_wod, u + 1)
            dve_norm(eng, 0)
        s_wot = sem("out_gated")

        ends["out"] = [(s_wod, 2 * LT), (s_l1, LT), (s_wo, 2 * LT)]

        hm = view(arena_a, 0, KT, L)
        comb = view(arena_t, 1024, LT, NE)
        s_hmT, s_hm = sem("stream_transposed"), sem("stream_modulated")
        s_lg, s_rt, s_re = sem("router_logits"), sem("router_steps"), sem("router_act_steps")

        def pe_turn_stream(eng, src, ready, at):
            for t in range(LT):
                ready(t)
                if t >= 2:
                    eng.wait_ge(s_hm, at + t - 1)
                for k in range(KT):
                    mm = eng.transpose(ps[:, 4 + 2 * (t % 2) + k // 4, (k % 4) * P:(k % 4 + 1) * P],
                                       src(t)[:, k * P:(k + 1) * P], ident[:, :])
                mm.then_inc(s_hmT, 1)

        def turned(t):
            return ps[:, 4 + 2 * (t % 2):6 + 2 * (t % 2), :].rearrange("p a (b n) -> p (a b) n", n=P)

        def pe_router(eng):
            pe_turn_stream(eng, lambda t: x1[:, t, :], lambda t: eng.wait_ge(s_l1, t + 1), 0)
            eng.wait_ge(s_wr, 32)
            eng.wait_ge(s_hm, LT)
            for t in range(LT):
                for k in range(KT):
                    mm = eng.matmul(ps[:, 3, t * 20:(t + 1) * 20], hm[:, k, t * P:(t + 1) * P], wr[:, k, :],
                                    start=(k == 0), stop=(k == KT - 1))
            mm.then_inc(s_lg, 1)
            eng.wait_ge(s_rt, 1)

        def act_router(eng):
            for t in range(LT):
                eng.wait_ge(s_hmT, t + 1)
                for k in range(KT):
                    ins = eng.activation(hm[:, k, t * P:(t + 1) * P], turned(t)[:, k, :], ACT.Identity,
                                         bias=modc[:, 3 * KT + k, 0:1], scale=modc[:, 4 * KT + k, 0:1])
                ins.then_inc(s_hm, 1)
            eng.wait_ge(s_rt, 3)
            eng.activation(gp, gl, ACT.Exp).then_inc(s_re, 1)
            eng.wait_ge(s_rt, N_RT_E)
            eng.activation(ew, ew, ACT.Exp).then_inc(s_re, 1)

        R0 = 1152
        lg = view(arena_t, R0, LT, MG + NE)
        gl = view(arena_t, R0 + 160, LT, MG)
        gp = view(arena_t, R0 + 192, LT, MG)
        goh = view(arena_t, R0 + 224, LT, MG)
        gmx = view(arena_t, R0 + 256, LT)
        gval = view(arena_t, R0 + 264, LT)
        esel = view(arena_t, R0 + 272, LT, EG)
        em1, em2 = view(arena_t, R0 + 304, LT), view(arena_t, R0 + 312, LT)
        oh1, oh2 = view(arena_t, R0 + 320, LT, EG), view(arena_t, R0 + 352, LT, EG)
        e2nd = view(arena_t, R0 + 384, LT, EG)
        ew = view(arena_t, R0 + 416, LT)
        w1, w2 = view(arena_t, R0 + 424, LT), view(arena_t, R0 + 432, LT)
        free_ = view(arena_t, R0 + 440, LT)
        tm4 = view(arena_t, R0 + 448, LT, EG)
        t16 = view(arena_t, R0 + 480, LT, NE)
        N_FIRST = 1 + 1 + 2 * (EG - 1)
        N_RT_E = 3 + 1 + N_FIRST + 2 + 1 + N_FIRST + 2 + 1 + 1

        def dve_router(eng):
            ch = Chain(eng, s_rt)
            eng.wait_ge(s_lg, 1)

            def first_of(oh, v, mx):
                ch(eng.tensor_tensor(oh, v, bc(mx, 2, EG), ALU.is_equal))
                ch(eng.tensor_scalar(free_, oh[:, :, 0], -1.0, 1.0, ALU.mult, ALU.add))
                for i in range(1, EG):
                    ch(eng.tensor_tensor(oh[:, :, i], oh[:, :, i], free_, ALU.mult))
                    ch(eng.tensor_tensor(free_, free_, oh[:, :, i], ALU.subtract))

            L3 = ps[:, 3, 0:LT * 20].rearrange("p (t n) -> p t n", n=20)
            eng.tensor_tensor(lg[:, :, 0:MG], L3[:, :, 0:MG], bc(rowv("b_rg"), 1, LT), ALU.add)
            ch(eng.tensor_tensor(lg[:, :, MG:], L3[:, :, MG:], bc(rowv("b_re"), 1, LT), ALU.add))
            ch(eng.tensor_reduce(gmx, lg[:, :, 0:MG], AX.X, ALU.max))
            ch(eng.tensor_tensor(gl, lg[:, :, 0:MG], bc(gmx, 2, MG), ALU.subtract))
            eng.wait_ge(s_re, 1)
            ch(eng.tensor_reduce(gval, gp, AX.X, ALU.add))
            first_of(goh, lg[:, :, 0:MG], gmx)
            el = lg[:, :, MG:].rearrange("p t (g e) -> p t g e", g=MG)
            ch(eng.tensor_tensor(t16.rearrange("p t (g e) -> p t g e", g=MG), el, bc(goh, 3, EG), ALU.mult))
            ch(eng.tensor_reduce(esel, t16.rearrange("p t (g e) -> p t e g", g=MG), AX.X, ALU.add))
            ch(eng.tensor_reduce(em1, esel, AX.X, ALU.max))
            first_of(oh1, esel, em1)
            ch(eng.tensor_scalar(tm4, oh1, -3.0e38, None, ALU.mult))
            ch(eng.tensor_tensor(e2nd, esel, tm4, ALU.add))
            ch(eng.tensor_reduce(em2, e2nd, AX.X, ALU.max))
            ch(eng.tensor_tensor(ew, em2, em1, ALU.subtract))
            assert ch.n == N_RT_E, (ch.n, N_RT_E)
            first_of(oh2, e2nd, em2)
            eng.wait_ge(s_re, 2)
            ch(eng.tensor_scalar(w1, ew, 1.0, None, ALU.add))
            ch(eng.tensor_tensor(w1, w1, gval, ALU.mult))
            ch(eng.reciprocal(w1, w1))
            ch(eng.tensor_tensor(w2, w1, ew, ALU.mult))
            ch(eng.tensor_tensor(oh1, oh1, bc(w1, 2, EG), ALU.mult))
            ch(eng.tensor_tensor(oh2, oh2, bc(w2, 2, EG), ALU.mult))
            ch(eng.tensor_tensor(oh1, oh1, oh2, ALU.add))
            ch(eng.tensor_tensor(comb.rearrange("p t (g e) -> p t g e", g=MG), bc(goh, 3, EG),
                                 bc(oh1, 2, MG), ALU.mult))
            N_RT.append(ch.n)

        N_RT = []

        acc_moe = view(arena_c, 0, LT, D)
        hid = [view(arena_d, i * 2 * L, 2, L) for i in range(2)]
        sil = [view(arena_t, i * HALF, HALF) for i in range(2)]
        BS = KT * 2 * FE + 2 * D

        gu_in = [sem(f"gate_up_loaded{i}") for i in range(2)]
        dn_in = [sem(f"down_loaded{i}") for i in range(2)]
        gu_done, silu_done, hid_done = sem("gate_up_product"), sem("silu_ready"), sem("hidden_ready")
        dn_done = sem("down_product")

        def swiglu(tag, before, blocks, hT, acc, w_gu, w_dn, scale_of, start, acc0, acc_done):
            guw = [view(ring, i * BS, KT, 2 * FE) for i in range(2)]
            dnw = [view(ring, i * BS + KT * 2 * FE, 2, D) for i in range(2)]
            NU, NM = 4, 2 * LT
            odd = blocks % 2
            G0, H0, M0 = before * 16, before * NU, before * NM
            full = (blocks - 1) // 2

            def load_gu(eng, b, s):
                g, u = w_gu(b)
                eng.dma_start(guw[s][:, :, 0:FE], g).then_inc(gu_in[s], 16)
                eng.dma_start(guw[s][:, :, FE:], u).then_inc(gu_in[s], 16)

            def load_dn(eng, b, s):
                eng.dma_start(dnw[s], w_dn(b)).then_inc(dn_in[s], 16)

            def sp(eng):
                start(eng)
                for s in range(2):
                    load_gu(eng, s, s)
                    load_dn(eng, s, s)

                def pair(b0, s):
                    eng.wait_ge(gu_done, (b0 + s - 1) * NU + H0)
                    load_gu(eng, b0 + s, s)
                    eng.wait_ge(dn_done, (b0 + s - 1) * NM + M0)
                    load_dn(eng, b0 + s, s)

                with eng.Fori(1, blocks // 2) as i:
                    for s in range(2):
                        pair(2 * i, s)
                if odd:
                    pair(blocks - 1, 0)

            def pe(eng):
                def gate_up(b, s, first=False):
                    eng.wait_ge(gu_in[s], (32 * (b // 2 + 1) if isinstance(b, int) else b[1]) + G0)
                    n = b if isinstance(b, int) else b[0]
                    for u in range(NU):
                        f, half = u % 2, u // 2
                        if not (first and u < 2):
                            eng.wait_ge(hid_done, n * NU + u - 1 + H0)
                        for w in range(2):
                            for k in range(KT):
                                mm = eng.matmul(ps[:, 2 * (u % 2) + w, :],
                                                guw[s][:, k, w * FE + f * P:w * FE + (f + 1) * P],
                                                hT[:, k, half * HALF:(half + 1) * HALF],
                                                start=(k == 0), stop=(k == KT - 1))
                        mm.then_inc(gu_done, 1)

                def down(b, s):
                    eng.wait_ge(dn_in[s], (16 * (b // 2 + 1) if isinstance(b, int) else b[1]) + G0 // 2)
                    n = b if isinstance(b, int) else b[0]
                    eng.wait_ge(hid_done, n * NU + NU + H0)
                    for m in range(NM):
                        t, h = m // 2, m % 2
                        eng.wait_ge(acc_done, n * NM + m + NM - 3)
                        for f in range(2):
                            mm = eng.matmul(ps[:, 4 + m % 4, :], hid[s][:, f, t * P:(t + 1) * P],
                                            dnw[s][:, f, h * HALF:(h + 1) * HALF],
                                            start=(f == 0), stop=(f == 1))
                        mm.then_inc(dn_done, 1)

                gate_up(0, 0, True)
                with eng.Fori(0, full) as i:
                    gate_up((2 * i + 1, 32 * i + 32), 1)
                    down((2 * i, 16 * i + 16), 0)
                    gate_up((2 * i + 2, 32 * i + 64), 0)
                    down((2 * i + 1, 16 * i + 16), 1)
                b = 2 * full
                if not odd:
                    gate_up(b + 1, 1)
                down(b, 0)
                if not odd:
                    down(b + 1, 1)

            def act(eng):
                def silu(n, first=False):
                    for u in range(NU):
                        eng.wait_ge(gu_done, n * NU + u + 1 + H0)
                        if not (first and u < 2):
                            eng.wait_ge(hid_done, n * NU + u - 1 + H0)
                        eng.activation(sil[u % 2], ps[:, 2 * (u % 2), :], ACT.Silu).then_inc(silu_done, 1)
                silu(0, True)
                with eng.Fori(1, blocks) as i:
                    silu(i)

            def dve(eng):
                def hidden(n, s):
                    for u in range(NU):
                        f, half = u % 2, u // 2
                        eng.wait_ge(silu_done, n * NU + u + 1 + H0)
                        eng.tensor_tensor(hid[s][:, f, half * HALF:(half + 1) * HALF], sil[u % 2],
                                          ps[:, 2 * (u % 2) + 1, :], ALU.mult).then_inc(hid_done, 1)

                def add(n):
                    for m in range(NM):
                        t, cs = m // 2, slice((m % 2) * HALF, (m % 2 + 1) * HALF)
                        eng.wait_ge(dn_done, n * NM + m + 1 + M0)
                        eng.wait_ge(acc_done, n * NM + m + 1)
                        o = acc[:, t, cs]
                        sc = scale_of(t, n)
                        if sc is None:
                            ins = eng.tensor_tensor(o, o, ps[:, 4 + m % 4, :], ALU.add)
                        else:
                            ins = eng.scalar_tensor_tensor(out=o, in0=ps[:, 4 + m % 4, :], scalar=sc, in1=o,
                                                           op0=ALU.mult, op1=ALU.add)
                        ins.then_inc(acc_done, 1)

                acc0(eng)
                hidden(0, 0)
                with eng.Fori(0, full) as i:
                    hidden(2 * i + 1, 1)
                    add(2 * i)
                    hidden(2 * i + 2, 0)
                    add(2 * i + 1)
                b = 2 * full
                if not odd:
                    hidden(b + 1, 1)
                add(b)
                if not odd:
                    add(b + 1)

            ends[tag] = [(acc_done, (blocks + 1) * NM), (dn_done, blocks * NM + M0), (gu_done, blocks * NU + H0)]
            return sp, pe, act, dve

        def gu_moe(b):
            return tuple(io[n][0][b].rearrange("(k p) f -> p k f", p=P) for n in ("w_gate", "w_up"))

        def dn_moe(b):
            return io["w_down"][0][b].rearrange("(f p) n -> p f n", p=P)

        s_moe = sem("moe_added")

        def acc0_moe(eng):
            after(eng, "out")
            for t in range(LT):
                for h in range(2):
                    eng.memset(acc_moe[:, t, h * HALF:(h + 1) * HALF], 0.0).then_inc(s_moe, 1)

        def start_moe(eng):
            eng.wait_ge(s_wo, 2 * LT)

        sp_moe, pe_moe, act_moe, dve_moe = swiglu(
            "moe", 0, NE, hm, acc_moe, gu_moe, dn_moe, lambda t, n: comb[:, t, bass.ds(n, 1)], start_moe, acc0_moe,
            s_moe)

        s_x2t, s_x2 = sem("experts_gated"), sem("experts_added")

        def sp_ln2(eng):
            eng.wait_ge(s_l1, LT)
            eng.dma_start(lng, io["ln2_g"][0].partition_broadcast(P)).then_inc(s_ln, 16)
            eng.dma_start(lnb, io["ln2_b"][0].partition_broadcast(P)).then_inc(s_ln, 16)

        def pe_x2(eng):
            after(eng, "moe")
            pe_row(eng, 5, 1)

        def dve_x2(eng):
            row_copy(eng, 1)
            for t in range(LT):
                step(eng, eng.tensor_tensor(acc_moe[:, t, :], acc_moe[:, t, :], rowg, ALU.mult), s_x2t, t + 1)
                eng.scalar_tensor_tensor(out=x1[:, t, :], in0=x1[:, t, :], scalar=ALPHA, in1=acc_moe[:, t, :],
                                         op0=ALU.mult, op1=ALU.add).then_inc(s_x2, 1)
            eng.wait_ge(s_x2, LT)
            dve_norm(eng, 1)

        ends["x2"] = [(s_l1, 2 * LT), (s_x2, LT)]

        ss8 = sb("ss8", [P, 3, LT])
        rr8 = sb("rr8", [P, 3, LT])
        xr = [view(arena_t, i * D, D) for i in range(2)]
        sqj = view(arena_t, 2 * D, D)
        s_ssq, s_rv, s_ra = sem("stream_squares"), sem("rms_steps"), sem("rms_roots")
        s_xr = sem("stream_normed")

        def act_rms(eng, i, *before):
            after(eng, *before)
            for t in range(LT):
                if i or t:
                    eng.wait_ge(s_ssq, LT * i + t)
                eng.activation(sqj, x1[:, t, :], ACT.Square, accum_out=ss8[:, i, t:t + 1]).then_inc(s_ssq, 1)
            eng.wait_ge(s_rv, 2 * i + 1)
            eng.activation(rr8[:, i, :], ss8[:, i, :], ACT.Sqrt).then_inc(s_ra, 1)

        def dve_rms(eng, i):
            ch = Chain(eng, s_rv, 2 * i)
            eng.wait_ge(s_ssq, LT * (i + 1))
            ch(eng.tensor_scalar(ss8[:, i, :], ss8[:, i, :], 1.0 / D, EPS_RMS, ALU.mult, ALU.add))
            eng.wait_ge(s_ra, i + 1)
            ch(eng.reciprocal(rr8[:, i, :], rr8[:, i, :]))

        def dve_normed(eng, i, dst, gain):
            for t in range(LT + 1):
                if t < LT:
                    if t >= 2 or i:
                        eng.wait_ge(s_hmT, LT * (i + 1) + t - 1)
                    eng.tensor_scalar(xr[t % 2], x1[:, t, :], rr8[:, i, t:t + 1], None, ALU.mult
                                      ).then_inc(s_xr, 1)
                if t >= 1:
                    eng.wait_ge(s_hmT, LT * (i + 1) + t)
                    eng.tensor_tensor(dst[:, :, (t - 1) * P:t * P], turned(t - 1), bc(col(gain), 2, P), ALU.mult
                                      ).then_inc(s_hm, 1)

        def pe_normed(eng, i):
            pe_turn_stream(eng, lambda t: xr[t % 2], lambda t: eng.wait_ge(s_xr, LT * i + t + 1), LT * (i + 1))

        hn = view(arena_a, 0, KT, L)
        ycat = view(arena_c, 0, KT, L)
        uc = view(arena_d, 0, G2, TC, SH)
        yc = view(arena_d, 4096, TC, HALF)
        PUW = 16
        pu = view(ring, 2 * PAN + 2048, PUW + L)
        pa, pb = view(arena_t, 0, PUW + L), view(arena_t, 1040, PUW + L)
        pd = view(arena_t, 2080, L)
        phead = view(arena_t, 3104, 4, 16)
        wpool = view(arena_t, 3168, 4, P)
        wglu = view(ring, 2 * PAN, 4, HALF)
        s_w2, s_wg2, s_wpl = [sem("in2_weights0"), sem("in2_weights1")], sem("glu_weights"), sem("pool_weights")
        s_wo2 = [sem("out2_weights0"), sem("out2_weights1")]
        s_b = sem("s5_b_loaded")
        s_pu, s_puc, s_puz = sem("pool_input"), sem("pool_input_copied"), sem("pool_zeroed")
        s_pdd, s_py, s_pyc = sem("pool_ready"), sem("pool_product"), sem("pool_scaled")
        s_u, s_uc = sem("s5_input"), sem("s5_input_copied")
        w_in2, w_out2 = io["w_in_2"][0], io["w_out_2"][0]
        bb1, bb2 = (view(arena_c, 8192 + 512 * i, G2, SH) for i in range(2))
        cc1, cc2 = (view(arena_c, 9216 + 512 * i, G2, SH) for i in range(2))

        def sp_second(eng):
            after(eng, "moe")
            for n in range(2):
                eng.dma_start(slot(n), panel_of(w_in2, 0, HALF * n)).then_inc(s_w2[n], 16)
            eng.dma_start(wglu, io["w_glu_2"][0].rearrange("(k p) n -> p k n", p=P)).then_inc(s_wg2, 16)
            for dst, lo, hi in ((bb1, "b_re_2", "b_im_2"), (bb2, "b_im_2", "b_re_2")):
                for a, n in ((0, lo), (SP2, hi)):
                    eng.dma_start(dst[a:a + SP2], io[n][0].rearrange("g p h -> p g h")).then_inc(s_b, 16)
            eng.wait_ge(s_hmT, 2 * LT)
            for m in range(4):
                eng.dma_start(phead[:, m, :], io["pool_heads"][m].partition_broadcast(P)).then_inc(s_wpl, 16)
            eng.dma_start(wpool, io["w_pool_2"][0].rearrange("g c d -> c g d")).then_inc(s_wpl, 16)

        def pe_second(eng):
            pe_normed(eng, 0)
            eng.wait_ge(s_hm, 2 * LT)
            eng.wait_ge(s_w2[1], 16)
            for t in range(TC):
                if t >= 2:
                    eng.wait_ge(s_uc, t - 1)
                for k in range(KT):
                    mm = eng.matmul(ps[:, t % 2, :], hn[:, k, t:L:TC], slot(1)[:, k, :],
                                    start=(k == 0), stop=(k == KT - 1))
                mm.then_inc(s_u, 1)
            eng.wait_ge(s_w2[0], 16)

            def pooled(m):
                eng.wait_ge(s_pdd, m + 1)
                for h in range(2):
                    if m >= 1:
                        eng.wait_ge(s_pyc, 2 * (m - 1) + h + 1)
                    eng.matmul(ps[:, 6 + h, :], wpool[:, m, :], pd[:, h * HALF:(h + 1) * HALF],
                               start=True, stop=True).then_inc(s_py, 1)

            for m in range(4):
                if m >= 2:
                    eng.wait_ge(s_puc, m - 1)
                for h in range(2):
                    for k in range(KT):
                        mm = eng.matmul(ps[:, 2 + 2 * (m % 2) + h, :], slot(0)[:, k, m * P:(m + 1) * P],
                                        hn[:, k, h * HALF:(h + 1) * HALF], start=(k == 0), stop=(k == KT - 1))
                mm.then_inc(s_pu, 1)
                if m == 0:
                    eng.wait_ge(s_wpl, 80)
                else:
                    pooled(m - 1)
            pooled(3)

        def act_second(eng):
            act_rms(eng, 0, "x2")
            for t in range(TC):
                eng.wait_ge(s_u, t + 1)
                eng.copy(uc[:, :, t, :], ps[:, t % 2, :].rearrange("p (g h) -> p g h", h=SH)).then_inc(s_uc, 1)
            eng.wait_ge(s_puz, 1)
            for m in range(5):
                if m < 4:
                    eng.wait_ge(s_pu, m + 1)
                    if m >= 1:
                        eng.wait_ge(s_pdd, m)
                    eng.copy(pu[:, PUW:], ps[:, 2 + 2 * (m % 2):4 + 2 * (m % 2), :].rearrange("p a n -> p (a n)")
                             ).then_inc(s_puc, 1)
                if m >= 1:
                    for h in range(2):
                        eng.wait_ge(s_py, 2 * (m - 1) + h + 1)
                        eng.activation(ycat[:, m - 1, h * HALF:(h + 1) * HALF], ps[:, 6 + h, :], ACT.Identity,
                                       scale=col("pool_scale_2")[:, m - 1:m]).then_inc(s_pyc, 1)

        def dve_second(eng):
            dve_rms(eng, 0)
            dve_normed(eng, 0, hn, "norm_mix_2")
            ch = Chain(eng, steps, chained[0])
            eng.wait_ge(s_hmT, 2 * LT)
            eng.memset(pu[:, 0:PUW], 0.0).then_inc(s_puz, 1)
            eng.wait_ge(s_wpl, 80)
            for m, width in enumerate(POOLS):
                eng.wait_ge(s_puc, m + 1)
                src, w, lo = pu, 1, 0
                while w < width:
                    dst = pa if src is not pa else pb
                    lo += w
                    n = PUW + L
                    ch(eng.tensor_tensor(dst[:, lo:n], src[:, lo:n], src[:, lo - w:n - w], ALU.add))
                    src, w = dst, 2 * w
                if m >= 1:
                    eng.wait_ge(s_py, 2 * m)
                ch(eng.scalar_tensor_tensor(out=pd, in0=src[:, PUW:], scalar=1.0 / width, in1=pu[:, PUW:],
                                            op0=ALU.mult, op1=ALU.subtract))
                ch(eng.tensor_tensor(pd[:, 0:16], src[:, PUW:PUW + 16], phead[:, m, :], ALU.mult))
                eng.tensor_tensor(pd[:, 0:16], pd[:, 0:16], pu[:, PUW:PUW + 16], ALU.subtract
                                  ).then_inc(s_pdd, 1)
            chained[0] = ch.n

        ends["second"] = [(s_uc, TC), (s_pyc, 8), (s_pdd, 4), (s_puc, 4), (s_py, 8)]

        RB = PAN
        ww = view(ring, RB, QG, 15, SH)
        prm = {}

        def par(name):
            if name not in prm:
                prm[name] = view(ring, RB + 1920 + 32 * len(prm), G2)
                assert 1920 + 32 * len(prm) <= PAN
            return prm[name]

        RC = 2 * PAN + 2048
        pwr, pwi, rvr, rvi = (view(ring, RC + 256 * i, G2, TC) for i in range(4))
        drow = view(ring, RC + 1024, HALF)
        bpr, bpi = (view(ring, RC + 1536 + 224 * i, 7, G2) for i in range(2))
        sgn = sb("sgn", [P, 1])
        jrot = m_gt
        cn = [view(arena_a, 512 * i, 4, P) for i in range(2)]
        lp = view(arena_a, 1024, 2, P)
        s_s5l, s_s5c, s_5c = sem("s5_loaded"), sem("s5_constants"), sem("s5_param_steps")
        s_5t, s_5a = sem("s5_params_transposed"), sem("s5_param_act_steps")

        def pool_s5_consts(eng):
            eng.wait_ge(s_diff, 4 * LT)
            eng.wait_ge(s_rr, 4 * LT)
            eng.memset(sgn[:, :], 1.0).then_inc(s_s5c, 1)
            eng.memset(jrot[:, :], 0.0).then_inc(s_s5c, 1)
            eng.wait_ge(s_s5c, 2)
            eng.affine_select(out=sgn[:, :], in_=sgn[:, :], compare_op=ALU.is_ge, fill=-1.0,
                              base=SP2 - 1, pattern=[[0, 1]], channel_multiplier=-1).then_inc(s_s5c, 1)
            eng.wait_ge(s_s5c, 3)
            for base, fill in ((-SP2, -1.0), (SP2, 1.0)):
                eng.affine_select(out=jrot[:, :], in_=jrot[:, :], compare_op=ALU.not_equal, fill=fill,
                                  base=base, pattern=[[-1, P]], channel_multiplier=1).then_inc(s_s5c, 1)
                eng.wait_ge(s_s5c, 4 if fill < 0 else 5)

        def sp_s5(eng):
            after(eng, "second")
            eng.wait_ge(s_hm, 2 * LT)
            eng.dma_start(slot(0), panel_of(w_out2, 0, 0)).then_inc(s_wo2[0], 16)
            for i, (a, b) in enumerate((("c_re_2", "c_im_2"), ("c_im_2", "c_re_2"))):
                for o, n in ((0, a), (SP2, b)):
                    eng.dma_start(cn[i][:, :, o:o + SP2], io[n][0].rearrange("(a g) h p -> (g h) a p", a=4)
                                  ).then_inc(s_s5l, 16)
            for i, n in enumerate(("lam_re_2", "lam_im_2")):
                for o in (0, SP2):
                    eng.dma_start(lp[0:G2, i, o:o + SP2], io[n][0]).then_inc(s_s5l, 16)
            eng.dma_start(par("ldt"), io["log_dt_2"][0].partition_broadcast(P)).then_inc(s_s5l, 16)
            eng.dma_start(drow, io["d_skip_2"][0].rearrange("g h -> (g h)").partition_broadcast(P)
                          ).then_inc(s_s5l, 16)

        def pe_s5_params(eng):
            eng.wait_ge(s_s5l, 160)
            after(eng, "second")
            for i in range(2):
                for a in range(4):
                    eng.transpose(ps[:, i, a * P:(a + 1) * P], cn[i][:, a, :], ident[:, :])
            for i in range(2):
                mm = eng.transpose(ps[:, 2, i * G2:(i + 1) * G2], lp[0:G2, i, :], ident[0:G2, 0:G2])
            mm.then_inc(s_5t, 1)

        TWO_PI = 6.283185307179586
        C_HI = 6.28125
        C_MID = float(np.float32(TWO_PI - C_HI))
        C_LO = TWO_PI - C_HI - C_MID
        MAGIC = 12582912.0

        def act_s5_params(eng):
            eng.wait_ge(s_s5l, 160)
            eng.activation(par("dt"), par("ldt"), ACT.Exp).then_inc(s_5a, 1)
            eng.wait_ge(s_5c, 5)
            eng.activation(par("mag0"), par("x"), ACT.Exp).then_inc(s_5a, 1)
            eng.wait_ge(s_5c, 11)
            eng.activation(par("sin"), par("r"), ACT.Sin).then_inc(s_5a, 1)
            eng.activation(par("sinh"), par("r"), ACT.Sin, scale=0.5).then_inc(s_5a, 1)

        def dve_s5_params(eng):
            ch = Chain(eng, s_5c)
            eng.wait_ge(s_5t, 1)
            eng.wait_ge(s_s5c, 5)
            eng.wait_ge(s_5a, 1)
            f = lambda v: v.rearrange("p g h -> p (g h)")

            def tt(o, a, b, op):
                ch(eng.tensor_tensor(o, a, b, op))

            def cmul(orr, oi, ar, ai, br, bi, t0, t1):
                tt(t0, ar, bi, ALU.mult)
                tt(t1, ai, br, ALU.mult)
                tt(t1, t0, t1, ALU.add)
                tt(t0, ai, bi, ALU.mult)
                tt(orr, ar, br, ALU.mult)
                tt(orr, orr, t0, ALU.subtract)
                ch(eng.tensor_copy(oi, t1))

            ch(eng.tensor_scalar(f(cc1), ps[:, 0, :], sgn[:, 0:1], None, ALU.mult))
            ch(eng.tensor_scalar(f(cc2), ps[:, 1, :], -1.0, None, ALU.mult))
            ch(eng.tensor_copy(par("lr"), ps[:, 2, 0:G2]))
            ch(eng.tensor_copy(par("li"), ps[:, 2, G2:2 * G2]))
            tt(par("x"), par("lr"), par("dt"), ALU.mult)
            tt(par("th"), par("li"), par("dt"), ALU.mult)
            ch(eng.tensor_scalar(par("n"), par("th"), 1.0 / TWO_PI, MAGIC, ALU.mult, ALU.add))
            ch(eng.tensor_scalar(par("n"), par("n"), MAGIC, None, ALU.subtract))
            ch(eng.scalar_tensor_tensor(out=par("r"), in0=par("n"), scalar=-C_HI, in1=par("th"),
                                        op0=ALU.mult, op1=ALU.add))
            ch(eng.scalar_tensor_tensor(out=par("r"), in0=par("n"), scalar=-C_MID, in1=par("r"),
                                        op0=ALU.mult, op1=ALU.add))
            ch(eng.tensor_scalar(par("r"), par("r"), 3.1415925, -3.1415925, ALU.min, ALU.max))
            eng.wait_ge(s_5a, 4)
            ch(eng.tensor_scalar(par("xc"), par("x"), 0.3, -0.3, ALU.min, ALU.max))
            tt(par("small"), par("x"), par("xc"), ALU.is_equal)
            ch(eng.tensor_scalar(par("q"), par("xc"), 1.0 / 6, 1.0, ALU.mult, ALU.add))
            for d in (5, 4, 3, 2):
                tt(par("q"), par("q"), par("xc"), ALU.mult)
                ch(eng.tensor_scalar(par("q"), par("q"), 1.0 / d, 1.0, ALU.mult, ALU.add))
            tt(par("q"), par("q"), par("xc"), ALU.mult)
            tt(par("q"), par("q"), par("small"), ALU.mult)
            ch(eng.tensor_scalar(par("small"), par("small"), -1.0, 1.0, ALU.mult, ALU.add))
            ch(eng.tensor_scalar(par("mag0"), par("mag0"), -1.0, None, ALU.add))
            tt(par("mag0"), par("mag0"), par("small"), ALU.mult)
            tt(par("q"), par("q"), par("mag0"), ALU.add)
            ch(eng.tensor_scalar(par("mag"), par("q"), 1.0, None, ALU.add))
            tt(par("cm"), par("sinh"), par("sinh"), ALU.mult)
            ch(eng.tensor_scalar(par("cm"), par("cm"), -2.0, None, ALU.mult))
            ch(eng.tensor_scalar(par("cos"), par("cm"), 1.0, None, ALU.add))
            tt(pwr[:, :, 0], par("mag"), par("cos"), ALU.mult)
            tt(pwi[:, :, 0], par("mag"), par("sin"), ALU.mult)
            tt(par("nr"), par("mag"), par("cm"), ALU.mult)
            tt(par("nr"), par("nr"), par("q"), ALU.add)
            tt(par("t0"), par("lr"), par("lr"), ALU.mult)
            tt(par("t1"), par("li"), par("li"), ALU.mult)
            tt(par("t0"), par("t0"), par("t1"), ALU.add)
            ch(eng.reciprocal(par("rden"), par("t0")))
            tt(par("t0"), par("nr"), par("lr"), ALU.mult)
            tt(par("t1"), pwi[:, :, 0], par("li"), ALU.mult)
            tt(par("t0"), par("t0"), par("t1"), ALU.add)
            tt(par("cr"), par("t0"), par("rden"), ALU.mult)
            tt(par("t0"), pwi[:, :, 0], par("lr"), ALU.mult)
            tt(par("t1"), par("nr"), par("li"), ALU.mult)
            tt(par("t0"), par("t0"), par("t1"), ALU.subtract)
            tt(par("ci"), par("t0"), par("rden"), ALU.mult)
            eng.wait_ge(s_b, 64)
            ch(eng.tensor_scalar(f(bb2), f(bb2), sgn[:, 0:1], -1.0, ALU.mult, ALU.mult))
            s0, s1, s2 = (view(arena_t, 512 * i, G2, SH) for i in range(3))
            tt(s0, bb1, bc(par("cr"), 2, SH), ALU.mult)
            tt(s1, bb2, bc(par("ci"), 2, SH), ALU.mult)
            tt(s0, s0, s1, ALU.add)
            tt(s1, bb2, bc(par("cr"), 2, SH), ALU.mult)
            tt(s2, bb1, bc(par("ci"), 2, SH), ALU.mult)
            tt(bb2, s1, s2, ALU.subtract)
            ch(eng.tensor_copy(bb1, s0))
            m = 1
            while m < TC:
                v = [a[:, :, 0:m] for a in (pwr, pwi)]
                w = [bc(a[:, :, m - 1], 2, m) for a in (pwr, pwi)]
                o = [a[:, :, m:2 * m] for a in (pwr, pwi)]
                t = [view(arena_t, 1536 + 128 * i, G2, 4)[:, :, 0:m] for i in range(2)]
                cmul(o[0], o[1], v[0], v[1], w[0], w[1], t[0], t[1])
                m *= 2
            for k in range(TC - 1):
                eng.tensor_copy(rvr[:, :, k], pwr[:, :, TC - 2 - k])
                ch(eng.tensor_copy(rvi[:, :, k], pwi[:, :, TC - 2 - k]))
            ch(eng.memset(rvr[:, :, TC - 1], 1.0))
            ch(eng.memset(rvi[:, :, TC - 1], 0.0))
            for k in range(3):
                tt(par("mag"), par("mag"), par("mag"), ALU.mult)
            ch(eng.tensor_copy(bpr[:, 0, :], par("cos")))
            ch(eng.tensor_copy(bpi[:, 0, :], par("sin")))
            for k in range(3):
                cmul(bpr[:, 0, :], bpi[:, 0, :], bpr[:, 0, :], bpi[:, 0, :], bpr[:, 0, :], bpi[:, 0, :],
                     par("t0"), par("t1"))
            tt(par("t0"), bpr[:, 0, :], bpr[:, 0, :], ALU.mult)
            tt(par("t1"), bpi[:, 0, :], bpi[:, 0, :], ALU.mult)
            tt(par("t0"), par("t0"), par("t1"), ALU.add)
            ch(eng.tensor_scalar(par("t0"), par("t0"), -0.5, 1.5, ALU.mult, ALU.add))
            tt(bpr[:, 0, :], bpr[:, 0, :], par("t0"), ALU.mult)
            tt(bpi[:, 0, :], bpi[:, 0, :], par("t0"), ALU.mult)
            for k in range(1, 7):
                cmul(bpr[:, k, :], bpi[:, k, :], bpr[:, k - 1, :], bpi[:, k - 1, :],
                     bpr[:, k - 1, :], bpi[:, k - 1, :], par("t0"), par("t1"))
            ch(eng.tensor_tensor(yc.rearrange("p t (g h) -> p g t h", h=SH), uc,
                                 bc(drow.rearrange("p (g h) -> p g h", h=SH), 2, TC), ALU.mult))
            ch(eng.memset(ww[:, :, TC:, :], 0.0))
            N_5C.append(ch.n)

        N_5C = []

        ee, ei, mt, cp, ut, vw, st = (view(arena_a, 1024 * i, QG, P) for i in range(7))
        sc1 = view(arena_a, 7168, QG, P)
        tsc, ctab, stab, sc2 = (view(arena_t, 1024 * i, QG, P) for i in range(4))
        q_names = ("u_turned", "e_turned", "inner", "inputs", "inputs_i", "states_i", "outputs")
        qp = {n: sem("s5_" + n) for n in q_names}
        qv = {n: sem("s5_" + n + "_used") for n in q_names}
        s_qw, s_qn = sem("s5_w_ready"), sem("s5_scanned")
        s_tab, s_tst, s_tbu = sem("s5_tables_ready"), sem("s5_table_steps"), sem("s5_tables_used")
        NQ = 4

        def pool_tables(eng):
            ch = Chain(eng, s_tst)
            for q in range(NQ):
                eng.wait_ge(s_5c, N_5C[0])
                gs = slice(q * QG, (q + 1) * QG)
                if q:
                    eng.wait_ge(s_tbu, q)
                ch(eng.memset(ctab[:, :, 0:1], 1.0))
                ch(eng.memset(stab[:, :, 0:1], 0.0))
                for k in range(7):
                    m = 1 << k
                    br, bi = bc(bpr[:, k, gs], 2, m), bc(bpi[:, k, gs], 2, m)
                    t = sc2[:, :, 0:m]
                    c0, s0, c1, s1 = ctab[:, :, 0:m], stab[:, :, 0:m], ctab[:, :, m:2 * m], stab[:, :, m:2 * m]
                    ch(eng.tensor_tensor(c1, c0, br, ALU.mult))
                    ch(eng.tensor_tensor(t, s0, bi, ALU.mult))
                    ch(eng.tensor_tensor(c1, c1, t, ALU.subtract))
                    ch(eng.tensor_tensor(s1, c0, bi, ALU.mult))
                    ch(eng.tensor_tensor(t, s0, br, ALU.mult))
                    ins = eng.tensor_tensor(s1, s1, t, ALU.add)
                    if k < 6:
                        ch(ins)
                ins.then_inc(s_tab, 1)

        def dve_quarters(eng):
            ch = Chain(eng, steps, chained[0])
            after(eng, "second")
            for q in range(NQ):
                gs = slice(q * QG, (q + 1) * QG)
                four = lambda v: v.rearrange("p g (t h) -> p g t h", h=SH)
                pair = lambda b: ps[:, b:b + 2, :].rearrange("p a (g n) -> p (a g) n", n=P)
                if q:
                    eng.wait_ge(qp["inner"], q)
                w8 = ww[:, :, 0:TC, :]
                ch(eng.tensor_tensor(w8, bc(rvr[:, gs, :], 3, SH), bc(bb1[:, gs, :], 2, TC), ALU.mult))
                ch(eng.tensor_tensor(four(sc1), bc(rvi[:, gs, :], 3, SH), bc(bb2[:, gs, :], 2, TC), ALU.mult))
                eng.tensor_tensor(w8, w8, four(sc1), ALU.add).then_inc(s_qw, 1)
                eng.wait_ge(qp["u_turned"], q + 1)
                if q:
                    eng.wait_ge(qp["outputs"], q)
                eng.tensor_copy(ut, pair(0)).then_inc(qv["u_turned"], 1)
                eng.wait_ge(qp["e_turned"], q + 1)
                ch(eng.tensor_copy(ee, pair(2)))
                eng.tensor_scalar(ei[:, :, 0:SP2], ee[:, :, SP2:], -1.0, None, ALU.mult)
                eng.tensor_copy(ei[:, :, SP2:], ee[:, :, 0:SP2]).then_inc(qv["e_turned"], 1)
                eng.wait_ge(qp["inner"], q + 1)
                eng.tensor_copy(mt, pair(4)).then_inc(qv["inner"], 1)
                eng.wait_ge(s_qw, q + 1)
                ch(eng.tensor_tensor(four(cp), bc(pwr[:, gs, :], 3, SH), bc(cc1[:, gs, :], 2, TC), ALU.mult))
                ch(eng.tensor_tensor(four(sc1), bc(pwi[:, gs, :], 3, SH), bc(cc2[:, gs, :], 2, TC), ALU.mult))
                ch(eng.tensor_tensor(four(cp), four(cp), four(sc1), ALU.add))
                eng.wait_ge(s_tab, q + 1)
                eng.wait_ge(qp["inputs"], q + 1)
                ch(eng.tensor_tensor(vw, pair(0), ctab, ALU.mult))
                eng.wait_ge(qp["inputs_i"], q + 1)
                ch(eng.tensor_tensor(sc1, pair(2), stab, ALU.mult))
                step(eng, eng.tensor_tensor(vw, vw, sc1, ALU.subtract), qv["inputs_i"], q + 1)
                for g in range(QG):
                    a = q * QG + g
                    ins = eng.tensor_tensor_scan(tsc[:, g, :], par("mag")[:, a:a + 1].to_broadcast([P, P]),
                                                 vw[:, g, :], 0.0, ALU.mult, ALU.add)
                step(eng, ins, s_qn, q + 1)
                ch(eng.tensor_tensor(st[:, :, 1:], tsc[:, :, 0:P - 1], ctab[:, :, 0:P - 1], ALU.mult))
                ch(eng.memset(st[:, :, 0:1], 0.0))
                eng.wait_ge(qp["states_i"], q + 1)
                ch(eng.tensor_tensor(sc1[:, :, 1:], pair(4)[:, :, 0:P - 1], stab[:, :, 0:P - 1], ALU.mult))
                step(eng, eng.tensor_tensor(st[:, :, 1:], st[:, :, 1:], sc1[:, :, 1:], ALU.add), s_tbu, q + 1)
                eng.wait_ge(qp["outputs"], q + 1)
                for b in range(2):
                    o = yc[:, :, q * P + b * HD:q * P + (b + 1) * HD].rearrange("p t (g h) -> p g t h", h=SH)
                    ins = eng.tensor_tensor(o, o, ps[:, 6 + b, :].rearrange("p (g t h) -> p g t h", g=4, h=SH),
                                            ALU.add)
                ins.then_inc(qv["outputs"], 1)

        def pe_quarters(eng):
            for q in range(NQ):
                def bank(b, g):
                    return ps[:, b + g // 4, (g % 4) * P:(g % 4 + 1) * P]
                if q == 0:
                    eng.wait_ge(s_5c, N_5C[0])
                for g in range(QG):
                    mm = eng.transpose(bank(0, g), uc[:, q * QG + g, :, :], ident[:, :])
                mm.then_inc(qp["u_turned"], 1)
                eng.wait_ge(s_qw, q + 1)
                for g in range(QG):
                    mm = eng.transpose(bank(2, g), ww[:, g, 0:TC, :], ident[:, :])
                mm.then_inc(qp["e_turned"], 1)
                if q:
                    eng.wait_ge(s_tbu, q)
                for g in range(QG):
                    for t in range(TC):
                        mm = eng.matmul(bank(4, g)[:, t * SH:(t + 1) * SH], ww[:, g, 7 - t:15 - t, :],
                                        cc1[:, q * QG + g, :], start=True, stop=True)
                mm.then_inc(qp["inner"], 1)
                eng.wait_ge(qv["u_turned"], q + 1)
                eng.wait_ge(qv["e_turned"], q + 1)
                for g in range(QG):
                    mm = eng.matmul(bank(0, g), ee[:, g, :], ut[:, g, :], start=True, stop=True)
                mm.then_inc(qp["inputs"], 1)
                for g in range(QG):
                    mm = eng.matmul(bank(2, g), ei[:, g, :], ut[:, g, :], start=True, stop=True)
                mm.then_inc(qp["inputs_i"], 1)
                eng.wait_ge(s_qn, q + 1)
                eng.wait_ge(qv["inner"], q + 1)
                for b in range(2):
                    mm = eng.matmul(ps[:, 4 + b, :], jrot[:, :],
                                    tsc[:, 4 * b:4 * b + 4, :].rearrange("p g n -> p (g n)"),
                                    start=True, stop=True)
                mm.then_inc(qp["states_i"], 1)
                eng.wait_ge(s_tbu, q + 1)
                if q:
                    eng.wait_ge(qv["outputs"], q)
                for g in range(QG):
                    eng.matmul(bank(6, g), ut[:, g, :], mt[:, g, :], start=True, stop=False)
                    mm = eng.matmul(bank(6, g), st[:, g, :], cp[:, g, :], start=False, stop=True)
                mm.then_inc(qp["outputs"], 1)

        yt = ycat[:, 4:8, :]
        sg = view(arena_d, 0, 4, L)
        s_ge, s_geT, s_gec = sem("gelu"), sem("gelu_transposed"), sem("gelu_copied")
        s_gz, s_sg, s_yg = sem("glu_product"), sem("glu_activated"), sem("glu_gated")

        def act_glu(eng):
            eng.wait_ge(qv["outputs"], NQ)
            for t in range(TC):
                eng.activation(yc[:, t, :], yc[:, t, :], ACT.Gelu_apprx_tanh).then_inc(s_ge, 1)
            for j in range(8):
                eng.wait_ge(s_gz, j + 1)
                m, h = j // 2, j % 2
                eng.activation(sg[:, m, h * HALF:(h + 1) * HALF], ps[:, 4 + j % 4, :], ACT.Sigmoid,
                               bias=col("b_glu_2")[:, m:m + 1]).then_inc(s_sg, 1)

        def pe_glu(eng):
            for t in range(TC):
                eng.wait_ge(s_ge, t + 1)
                if t >= 2:
                    eng.wait_ge(s_gec, t - 1)
                for k in range(4):
                    mm = eng.transpose(ps[:, t % 2, k * P:(k + 1) * P], yc[:, t, k * P:(k + 1) * P], ident[:, :])
                mm.then_inc(s_geT, 1)
            eng.wait_ge(s_gec, TC)
            eng.wait_ge(s_wg2, 16)
            eng.wait_ge(qv["outputs"], NQ)
            for j in range(8):
                m, h = j // 2, j % 2
                if j >= 4:
                    eng.wait_ge(s_sg, j - 3)
                for k in range(4):
                    mm = eng.matmul(ps[:, 4 + j % 4, :], wglu[:, k, m * P:(m + 1) * P],
                                    yt[:, k, h * HALF:(h + 1) * HALF], start=(k == 0), stop=(k == 3))
                mm.then_inc(s_gz, 1)

        def dve_glu(eng):
            for t in range(TC):
                eng.wait_ge(s_geT, t + 1)
                eng.tensor_copy(yt[:, :, t:L:TC], ps[:, t % 2, :].rearrange("p (k n) -> p k n", n=P)
                                ).then_inc(s_gec, 1)
            eng.wait_ge(s_gz, 8)
            for k in range(4):
                eng.wait_ge(s_sg, 2 * k + 2)
                eng.tensor_tensor(yt[:, k, :], yt[:, k, :], sg[:, k, :], ALU.mult).then_inc(s_yg, 1)

        s_o2 = sem("out2_product")
        s_ffn = sem("ffn_added")
        ends["h2"] = [(s_ffn, 2 * LT)]

        def sp_out2(eng):
            eng.wait_ge(qp["outputs"], NQ)
            eng.wait_ge(qv["outputs"], NQ)
            eng.dma_start(slot(1), panel_of(w_out2, 0, HALF)).then_inc(s_wo2[1], 16)

        def pe_out2(eng):
            eng.wait_ge(s_yg, 4)
            eng.wait_ge(s_sg, 8)
            for n in range(2):
                eng.wait_ge(s_wo2[n], 16)
                for t in range(LT):
                    u = n * LT + t
                    if u >= 4:
                        eng.wait_ge(s_ffn, u - 3)
                    for k in range(KT):
                        mm = eng.matmul(ps[:, u % 4, :], ycat[:, k, t * P:(t + 1) * P], slot(n)[:, k, :],
                                        start=(k == 0), stop=(k == KT - 1))
                    mm.then_inc(s_o2, 1)

        def dve_out2(eng):
            for u in range(2 * LT):
                n, t = u // LT, u % LT
                cs = slice(n * HALF, (n + 1) * HALF)
                eng.wait_ge(s_o2, u + 1)
                eng.tensor_tensor(x1[:, t, cs], x1[:, t, cs], ps[:, u % 4, :], ALU.add).then_inc(s_ffn, 1)
            eng.wait_ge(s_ffn, 2 * LT)
            dve_rms(eng, 1)
            dve_normed(eng, 1, hn, "norm_ffn_2")

        def gu_ffn(b):
            return tuple(io[n][0].rearrange("(k p) (b f) -> b p k f", p=P, f=FE)[b]
                         for n in ("w_gate_2", "w_up_2"))

        def dn_ffn(b):
            return io["w_down_2"][0].rearrange("(b f p) n -> b p f n", f=2, p=P)[b]

        sp_ffn, pe_ffn, act_ffn, dve_ffn = swiglu(
            "ffn", NE, FB, hn, x1, gu_ffn, dn_ffn, lambda t, n: None, lambda eng: eng.wait_ge(s_o2, 2 * LT),
            lambda eng: None, s_ffn)

        rowf = view(arena_d, 0, D)
        s_rowf, s_fin, s_out = sem("final_gain_loaded"), sem("final_normed"), sem("output_stored")

        def sp_final(eng):
            after(eng, "ffn")
            eng.dma_start(rowf, io["norm_final_2"].partition_broadcast(P)).then_inc(s_rowf, 16)
            for t in range(LT):
                eng.wait_ge(s_fin, t + 1)
                eng.dma_start(out[t * P:(t + 1) * P, :], x1[:, t, :]).then_inc(s_out, 16)
            eng.wait_ge(s_out, 16 * LT)

        def dve_final(eng):
            dve_rms(eng, 2)
            eng.wait_ge(s_rowf, 16)
            for t in range(LT):
                eng.scalar_tensor_tensor(out=x1[:, t, :], in0=x1[:, t, :], scalar=rr8[:, 2, t:t + 1], in1=rowf,
                                         op0=ALU.mult, op1=ALU.mult).then_inc(s_fin, 1)

        block = ctx.enter_context(nc.Block())

        @block.vector
        def _(eng):
            dve_pack(eng)
            dve_mod(eng, 0, 0, 16)
            hx_evac(eng, "dve")
            dve_conv(eng)
            dve_dt(eng)
            dve_ssd(eng)
            dve_gate(eng)
            dve_qkv(eng)
            dve_mod2(eng)
            dve_att(eng)
            dve_out(eng)
            dve_router(eng)
            dve_moe(eng)
            dve_x2(eng)
            dve_second(eng)
            dve_s5_params(eng)
            dve_quarters(eng)
            dve_glu(eng)
            dve_out2(eng)
            dve_ffn(eng)
            dve_final(eng)

        @block.sync
        def _(eng):
            sp_first(eng)
            sp_gate(eng)
            sp_out(eng)
            sp_ln2(eng)
            sp_moe(eng)
            sp_second(eng)
            sp_s5(eng)
            sp_out2(eng)
            sp_ffn(eng)
            sp_final(eng)

        @block.gpsimd
        def _(eng):
            pool_consts(eng)
            pool_ssd(eng)
            pool_s5_consts(eng)
            pool_tables(eng)

        @block.scalar
        def _(eng):
            act_small(eng)
            act_silu_c(eng)
            hx_evac(eng, "act")
            act_xbc(eng)
            act_dt(eng)
            act_ssd(eng)
            act_gate(eng)
            act_qkv(eng)
            act_att(eng)
            act_norm(eng, 0)
            act_router(eng)
            act_moe(eng)
            act_norm(eng, 1)
            act_second(eng)
            act_s5_params(eng)
            act_glu(eng)
            act_rms(eng, 1, "h2")
            act_ffn(eng)
            act_rms(eng, 2, "ffn")

        @block.tensor
        def _(eng):
            pe_pack(eng)
            pe_mod(eng, 0, 0, 0, 16)
            pe_hx(eng)
            pe_xbc(eng)
            pe_dt(eng)
            pe_ssd(eng)
            pe_gate(eng)
            pe_qkv(eng)
            pe_mod2(eng)
            pe_att(eng)
            pe_out(eng)
            pe_router(eng)
            pe_moe(eng)
            pe_x2(eng)
            pe_second(eng)
            pe_s5_params(eng)
            pe_quarters(eng)
            pe_glu(eng)
            pe_out2(eng)
            pe_normed(eng, 1)
            eng.wait_ge(s_hm, 3 * LT)
            pe_ffn(eng)


def kernel(**inputs):
    import concourse.bacc as bacc
    from concourse.bass_utils import run_bass_kernel_spmd as run

    nc = bacc.Bacc("TRN2", target_bir_lowering=False, num_devices=1)
    arrays = {name: np.ascontiguousarray(a) for name, a in inputs.items()}

    inv_freq = (10000.0 ** (-np.arange(0, 32, 2, dtype=np.float32) / 32.0)).astype(np.float32)
    tok = np.arange(L)
    ang = np.concatenate([(tok // 64).astype(np.float32)[:, None] * inv_freq,
                          (tok % 64).astype(np.float32)[:, None] * inv_freq], -1)
    arrays["rope_table"] = np.stack([np.cos(ang), np.sin(ang)]).astype(np.float32)
    arrays["pool_heads"] = np.stack([1.0 / np.minimum(np.arange(1, 17), w) for w in POOLS]).astype(np.float32)

    io = {name: nc.dram_tensor("in_" + name, a.shape, F32, kind="ExternalInput").ap()
          for name, a in arrays.items()}
    out = nc.dram_tensor("out", [L, D], F32, kind="ExternalOutput").ap()
    build(nc, io, out)
    r = run(nc, [{"in_" + name: a for name, a in arrays.items()}], core_ids=[0])
    return r.results[0]["out"].reshape(1, L, D)
```
